# Optimizing a Trainium2 kernel written in Bass

```python
import math
import jax
import jax.numpy as jnp
from jax import lax
import numpy as np

D_MODEL = 1024
BATCH = 1
SEQ = 256
DEPTH = 2

GRID_W = 64
CTX_LEN = 256
HEAD_DIM = 64
MIX_W = D_MODEL
Q_BLOCK = 128
ROPE_THETA = 10000.0
DIFF_HEADS = MIX_W // 2 // (2 * HEAD_DIM)
DIFF_QK = DIFF_HEADS * 2 * HEAD_DIM
DIFF_V = DIFF_HEADS * 2 * HEAD_DIM
GQA_HEADS = MIX_W // 2 // HEAD_DIM
GQA_KV_HEADS = max(1, GQA_HEADS // 4)
GQA_GROUP = GQA_HEADS // GQA_KV_HEADS
GQA_Q = GQA_HEADS * HEAD_DIM
GQA_KV_W = GQA_KV_HEADS * HEAD_DIM
AB_Q = DIFF_QK + GQA_Q
AB_KV = DIFF_QK + DIFF_V + 2 * GQA_KV_W
AB_OUT = DIFF_V + GQA_Q
WINDOW = 128
WIN_HEADS = MIX_W // 2 // HEAD_DIM
WIN_KV_HEADS = max(1, WIN_HEADS // 4)
WIN_GROUP = WIN_HEADS // WIN_KV_HEADS
WIN_Q = WIN_HEADS * HEAD_DIM
WIN_KV_W = WIN_KV_HEADS * HEAD_DIM
NA_HEADS = MIX_W // 2 // HEAD_DIM
NA_W = NA_HEADS * HEAD_DIM
NA_ROWS_MAX = 8
NA_COLS = 16
CD_Q = WIN_Q + NA_W
CD_KV = 2 * WIN_KV_W + 2 * NA_W
CD_OUT = WIN_Q + NA_W
N_GROUPS = 4
EXPERTS_PER_GROUP = 8
N_EXPERTS = N_GROUPS * EXPERTS_PER_GROUP
TOP_K_IN_GROUP = 2
D_EXPERT = D_MODEL // 2
MOE_BLOCK = 128
N_EVEN = (DEPTH + 1) // 2
N_ODD = DEPTH // 2
ALPHA = (2.0 * DEPTH) ** 0.25
BETA = (8.0 * DEPTH) ** -0.25
LN_EPS = 1e-5
RMS_EPS = 1e-6
ATTN_SCALE = HEAD_DIM ** -0.5
NEG_INF = -1e30


def layer_norm(x, g, b):
    xf = x.astype(jnp.float32)
    mu = jnp.mean(xf, -1, keepdims=True)
    var = jnp.mean(jnp.square(xf - mu), -1, keepdims=True)
    y = (xf - mu) * lax.rsqrt(var + LN_EPS) * g.astype(jnp.float32) + b.astype(jnp.float32)
    return y.astype(x.dtype)

def rms_norm(x, g):
    xf = x.astype(jnp.float32)
    y = xf * lax.rsqrt(jnp.mean(jnp.square(xf), -1, keepdims=True) + RMS_EPS) * g.astype(jnp.float32)
    return y.astype(x.dtype)

def modulate(x, shift, scale):
    return x * (1.0 + scale) + shift

def lambda_init(layer_idx):
    return 0.8 - 0.6 * math.exp(-0.3 * layer_idx)

def axial_rope_tables(n_tokens):
    t = jnp.arange(n_tokens, dtype=jnp.int32)
    row = (t // GRID_W).astype(jnp.float32)
    col = (t % GRID_W).astype(jnp.float32)
    n_freq = HEAD_DIM // 4
    inv = ROPE_THETA ** (-jnp.arange(n_freq, dtype=jnp.float32) / n_freq)
    ang = jnp.concatenate([row[:, None] * inv, col[:, None] * inv], -1)
    return jnp.cos(ang), jnp.sin(ang)

def apply_rope(x, cos, sin):
    shp = (1, cos.shape[0]) + (1,) * (x.ndim - 3) + (cos.shape[1],)
    cos = cos.reshape(shp)
    sin = sin.reshape(shp)
    xf = x.astype(jnp.float32)
    x1, x2 = jnp.split(xf, 2, -1)
    return jnp.concatenate([x1 * cos - x2 * sin, x2 * cos + x1 * sin], -1).astype(x.dtype)

def sweep_query_blocks(fn, q):
    b, s = q.shape[:2]
    nb = s // Q_BLOCK
    qb = jnp.moveaxis(q.reshape((b, nb, Q_BLOCK) + q.shape[2:]), 1, 0)
    out = lax.map(lambda a: fn(a[0], a[1]), (jnp.arange(nb, dtype=jnp.int32), qb))
    out = jnp.moveaxis(out, 0, 1)
    return out.reshape((b, s) + out.shape[3:])

def diff_attend(qb, k, v, lam):
    s = jnp.einsum('bqhcd,bkhcd->bhcqk', qb, k).astype(jnp.float32) * ATTN_SCALE
    p = jax.nn.softmax(s, -1)
    a = p[:, :, 0] - lam * p[:, :, 1]
    return jnp.einsum('bhqk,bkhe->bqhe', a.astype(v.dtype), v)

def gqa_attend(qb, k, v):
    s = jnp.einsum('bqhgd,bkhd->bhgqk', qb, k).astype(jnp.float32) * ATTN_SCALE
    p = jax.nn.softmax(s, -1)
    return jnp.einsum('bhgqk,bkhd->bqhgd', p.astype(v.dtype), v)

def sink_attend(qb, k, v, sink, valid=None):
    s = jnp.einsum('bqhgd,bkhd->bhgqk', qb, k).astype(jnp.float32) * ATTN_SCALE
    if valid is not None:
        s = jnp.where(valid, s, NEG_INF)
    sk = jnp.broadcast_to(sink.astype(jnp.float32)[None, :, :, None, None], s.shape[:-1] + (1,))
    p = jax.nn.softmax(jnp.concatenate([s, sk], -1), -1)[..., :-1]
    return jnp.einsum('bhgqk,bkhd->bqhgd', p.astype(v.dtype), v)

def window_attention(q, k, v, kc, vc, sink):
    s = q.shape[1]
    n_ctx = kc.shape[1]
    span = Q_BLOCK + 2 * WINDOW
    pad = ((0, 0), (WINDOW, WINDOW), (0, 0), (0, 0))
    kp = jnp.pad(k, pad)
    vp = jnp.pad(v, pad)
    ctx_valid = jnp.ones((Q_BLOCK, n_ctx), dtype=bool)

    def block(bi, qb):
        start = bi * Q_BLOCK
        kb = lax.dynamic_slice_in_dim(kp, start, span, axis=1)
        vb = lax.dynamic_slice_in_dim(vp, start, span, axis=1)
        qpos = start + jnp.arange(Q_BLOCK)
        kpos = start - WINDOW + jnp.arange(span)
        local = (jnp.abs(qpos[:, None] - kpos[None, :]) <= WINDOW) & (kpos >= 0)[None, :] & (kpos < s)[None, :]
        valid = jnp.concatenate([local, ctx_valid], 1)
        return sink_attend(qb, jnp.concatenate([kb, kc], 1), jnp.concatenate([vb, vc], 1), sink, valid)

    return sweep_query_blocks(block, q)

def neighbourhood_attention(q, k, v, kc, vc, rpb):
    b, s, h, d = q.shape
    rows = s // GRID_W
    kr = min(NA_ROWS_MAX, rows)
    n_nb = kr * NA_COLS
    qg = jnp.moveaxis(q.reshape(b, rows, GRID_W, h, d), 1, 0)
    kg = k.reshape(b, rows, GRID_W, h, d)
    vg = v.reshape(b, rows, GRID_W, h, d)
    col = jnp.arange(GRID_W)
    col_start = jnp.clip(col - NA_COLS // 2, 0, GRID_W - NA_COLS)
    cols = col_start[:, None] + jnp.arange(NA_COLS)
    col_off = cols - col[:, None] + (NA_COLS - 1)

    def row_block(a):
        r, qr = a
        r0 = jnp.clip(r - kr // 2, 0, rows - kr)
        slab_k = lax.dynamic_slice_in_dim(kg, r0, kr, axis=1)
        slab_v = lax.dynamic_slice_in_dim(vg, r0, kr, axis=1)
        k_nb = jnp.moveaxis(slab_k[:, :, cols], 1, 2).reshape(b, GRID_W, n_nb, h, d)
        v_nb = jnp.moveaxis(slab_v[:, :, cols], 1, 2).reshape(b, GRID_W, n_nb, h, d)
        row_off = r0 + jnp.arange(kr) - r + (NA_ROWS_MAX - 1)
        bias = rpb[:, row_off[None, :, None], col_off[:, None, :]].reshape(h, GRID_W, n_nb)
        s_nb = jnp.einsum('bqhd,bqkhd->bhqk', qr, k_nb).astype(jnp.float32) * ATTN_SCALE + bias.astype(jnp.float32)[None]
        s_cx = jnp.einsum('bqhd,bkhd->bhqk', qr, kc).astype(jnp.float32) * ATTN_SCALE
        p = jax.nn.softmax(jnp.concatenate([s_nb, s_cx], -1), -1).astype(v.dtype)
        return (jnp.einsum('bhqk,bqkhd->bqhd', p[..., :n_nb], v_nb)
                + jnp.einsum('bhqk,bkhd->bqhd', p[..., n_nb:], vc))

    out = lax.map(row_block, (jnp.arange(rows, dtype=jnp.int32), qg))
    return jnp.moveaxis(out, 0, 1).reshape(b, s, h, d)

def mixer_ab(a_lat, a_ctx, ctx_kv_only, w_in, w_out, lam_vecs, subln_g, qk_g, lam_init, cos, sin):
    b = a_lat.shape[0]

    def split_q(p):
        n = p.shape[1]
        q_d = p[..., :DIFF_QK].reshape(b, n, DIFF_HEADS, 2, HEAD_DIM)
        q_g = rms_norm(p[..., DIFF_QK:AB_Q].reshape(b, n, GQA_KV_HEADS, GQA_GROUP, HEAD_DIM), qk_g[0])
        return q_d, q_g

    def split_kv(p):
        n = p.shape[1]
        o1 = DIFF_QK
        o2 = o1 + DIFF_V
        o3 = o2 + GQA_KV_W
        k_d = p[..., :o1].reshape(b, n, DIFF_HEADS, 2, HEAD_DIM)
        v_d = p[..., o1:o2].reshape(b, n, DIFF_HEADS, 2 * HEAD_DIM)
        k_g = rms_norm(p[..., o2:o3].reshape(b, n, GQA_KV_HEADS, HEAD_DIM), qk_g[1])
        v_g = p[..., o3:].reshape(b, n, GQA_KV_HEADS, HEAD_DIM)
        return k_d, v_d, k_g, v_g

    lv = lam_vecs.astype(jnp.float32)
    lam = jnp.exp(jnp.sum(lv[0] * lv[1])) - jnp.exp(jnp.sum(lv[2] * lv[3])) + lam_init

    p_lat = a_lat @ w_in
    q_d, q_g = split_q(p_lat[..., :AB_Q])
    k_d, v_d, k_g, v_g = split_kv(p_lat[..., AB_Q:])
    q_d, k_d, q_g, k_g = (apply_rope(t, cos, sin) for t in (q_d, k_d, q_g, k_g))
    if ctx_kv_only:
        ck_d, cv_d, ck_g, cv_g = split_kv(a_ctx @ w_in[:, AB_Q:])
    else:
        p_ctx = a_ctx @ w_in
        cq_d, cq_g = split_q(p_ctx[..., :AB_Q])
        ck_d, cv_d, ck_g, cv_g = split_kv(p_ctx[..., AB_Q:])

    kd_all = jnp.concatenate([k_d, ck_d], 1)
    vd_all = jnp.concatenate([v_d, cv_d], 1)
    kg_all = jnp.concatenate([k_g, ck_g], 1)
    vg_all = jnp.concatenate([v_g, cv_g], 1)
    o_d = sweep_query_blocks(lambda _, qb: diff_attend(qb, kd_all, vd_all, lam), q_d)
    o_g = sweep_query_blocks(lambda _, qb: gqa_attend(qb, kg_all, vg_all), q_g)

    def merge(od, og):
        n = od.shape[1]
        od = rms_norm(od, subln_g) * (1.0 - lam_init)
        return jnp.concatenate([od.reshape(b, n, DIFF_V), og.reshape(b, n, GQA_Q)], -1) @ w_out

    out_lat = merge(o_d, o_g)
    if ctx_kv_only:
        return out_lat, None
    out_ctx = merge(diff_attend(cq_d, ck_d, cv_d, lam), gqa_attend(cq_g, ck_g, cv_g))
    return out_lat, out_ctx

def mixer_cd(a_lat, a_ctx, ctx_kv_only, w_in, w_out, sink, rpb, cos, sin):
    b = a_lat.shape[0]
    sink_hg = sink.reshape(WIN_KV_HEADS, WIN_GROUP)

    def split_q(p):
        n = p.shape[1]
        q_w = p[..., :WIN_Q].reshape(b, n, WIN_KV_HEADS, WIN_GROUP, HEAD_DIM)
        q_n = p[..., WIN_Q:CD_Q].reshape(b, n, NA_HEADS, HEAD_DIM)
        return q_w, q_n

    def split_kv(p):
        n = p.shape[1]
        o1 = WIN_KV_W
        o2 = o1 + WIN_KV_W
        o3 = o2 + NA_W
        k_w = p[..., :o1].reshape(b, n, WIN_KV_HEADS, HEAD_DIM)
        v_w = p[..., o1:o2].reshape(b, n, WIN_KV_HEADS, HEAD_DIM)
        k_n = p[..., o2:o3].reshape(b, n, NA_HEADS, HEAD_DIM)
        v_n = p[..., o3:].reshape(b, n, NA_HEADS, HEAD_DIM)
        return k_w, v_w, k_n, v_n

    p_lat = a_lat @ w_in
    q_w, q_n = split_q(p_lat[..., :CD_Q])
    k_w, v_w, k_n, v_n = split_kv(p_lat[..., CD_Q:])
    q_w = apply_rope(q_w, cos, sin)
    k_w = apply_rope(k_w, cos, sin)
    if ctx_kv_only:
        ck_w, cv_w, ck_n, cv_n = split_kv(a_ctx @ w_in[:, CD_Q:])
    else:
        p_ctx = a_ctx @ w_in
        cq_w, cq_n = split_q(p_ctx[..., :CD_Q])
        ck_w, cv_w, ck_n, cv_n = split_kv(p_ctx[..., CD_Q:])

    o_w = window_attention(q_w, k_w, v_w, ck_w, cv_w, sink_hg)
    o_n = neighbourhood_attention(q_n, k_n, v_n, ck_n, cv_n, rpb)

    def merge(ow, on):
        n = ow.shape[1]
        return jnp.concatenate([ow.reshape(b, n, WIN_Q), on.reshape(b, n, NA_W)], -1) @ w_out

    out_lat = merge(o_w, o_n)
    if ctx_kv_only:
        return out_lat, None
    n_ctx = a_ctx.shape[1]
    co_w = sink_attend(cq_w, ck_w, cv_w, sink_hg)
    co_n = gqa_attend(cq_n.reshape(b, n_ctx, NA_HEADS, 1, HEAD_DIM), ck_n, cv_n)
    return out_lat, merge(co_w, co_n)

def hier_moe(h, w_group, b_group, w_router, b_router, w1, w3, w2):
    t, d = h.shape
    g_logits = (h @ w_group).astype(jnp.float32) + b_group.astype(jnp.float32)
    _, g_idx = lax.top_k(g_logits, 1)
    g_w = jnp.take_along_axis(jax.nn.softmax(g_logits, -1), g_idx, -1)
    e_logits = ((h @ w_router).astype(jnp.float32) + b_router.astype(jnp.float32)).reshape(t, N_GROUPS, EXPERTS_PER_GROUP)
    e_in = jnp.take_along_axis(e_logits, g_idx[:, :, None], 1)[:, 0]
    top_v, top_i = lax.top_k(e_in, TOP_K_IN_GROUP)
    weights = g_w * jax.nn.softmax(top_v, -1)
    experts = g_idx * EXPERTS_PER_GROUP + top_i

    n_assign = t * TOP_K_IN_GROUP
    e_flat = experts.reshape(n_assign)
    tok = jnp.repeat(jnp.arange(t, dtype=jnp.int32), TOP_K_IN_GROUP)
    w_flat = weights.reshape(n_assign)
    order = jnp.argsort(e_flat)
    e_s = e_flat[order]
    tok_s = tok[order]
    w_s = w_flat[order]
    counts = jnp.bincount(e_flat, length=N_EXPERTS)
    starts = jnp.cumsum(counts) - counts
    padded = (counts + MOE_BLOCK - 1) // MOE_BLOCK * MOE_BLOCK
    p_ends = jnp.cumsum(padded)
    p_starts = p_ends - padded
    dest = p_starts[e_s] + (jnp.arange(n_assign, dtype=jnp.int32) - starts[e_s])
    n_blocks = (n_assign + MOE_BLOCK - 1) // MOE_BLOCK + N_EXPERTS
    buf = jnp.zeros((n_blocks * MOE_BLOCK, d), h.dtype).at[dest].set(h[tok_s])
    blk_e = jnp.minimum(jnp.searchsorted(p_ends, jnp.arange(n_blocks) * MOE_BLOCK, side='right'), N_EXPERTS - 1)

    def expert_block(a):
        xb, e = a
        return (jax.nn.silu(xb @ w1[e]) * (xb @ w3[e])) @ w2[e]

    yb = lax.map(expert_block, (buf.reshape(n_blocks, MOE_BLOCK, d), blk_e)).reshape(n_blocks * MOE_BLOCK, d)
    return jnp.zeros((t, d), h.dtype).at[tok_s].add(w_s[:, None].astype(h.dtype) * yb[dest])

def first_inputs(seed: int = 0) -> dict:
    key = jax.random.key(seed)
    ks = jax.random.split(key, 32)
    D = D_MODEL

    def nrm(k, shape, s):
        return jax.random.normal(k, shape, jnp.float32) * s

    ab_kv_scale = jnp.concatenate([jnp.ones((DIFF_QK,)), jnp.full((DIFF_V,), BETA), jnp.ones((GQA_KV_W,)), jnp.full((GQA_KV_W,), BETA)]).astype(jnp.float32)
    cd_kv_scale = jnp.concatenate([jnp.ones((WIN_KV_W,)), jnp.full((WIN_KV_W,), BETA), jnp.ones((NA_W,)), jnp.full((NA_W,), BETA)]).astype(jnp.float32)
    return {
        'x': nrm(ks[0], (BATCH, SEQ, D), 1.0),
        'c': nrm(ks[1], (BATCH, D), 1.0),
        'ctx': nrm(ks[2], (BATCH, CTX_LEN, D), 1.0),
        'c_ctx': nrm(ks[3], (D,), 1.0),
        'mod_w': nrm(ks[4], (DEPTH, D, 6 * D), 0.5 * D ** -0.5),
        'mod_b': nrm(ks[5], (DEPTH, 6 * D), 0.02),
        'ln_g': 1.0 + nrm(ks[6], (DEPTH, 2, D), 0.02),
        'ln_b': nrm(ks[7], (DEPTH, 2, D), 0.02),
        'ab_w_in': jnp.concatenate([nrm(ks[8], (N_EVEN, D, AB_Q), D ** -0.5), nrm(ks[9], (N_EVEN, D, AB_KV), D ** -0.5) * ab_kv_scale], -1),
        'ab_w_out': nrm(ks[10], (N_EVEN, AB_OUT, D), AB_OUT ** -0.5 * BETA),
        'diff_lambda': nrm(ks[11], (N_EVEN, 4, HEAD_DIM), 0.1),
        'diff_subln_g': 1.0 + nrm(ks[12], (N_EVEN, 2 * HEAD_DIM), 0.02),
        'gqa_qk_g': 1.0 + nrm(ks[13], (N_EVEN, 2, HEAD_DIM), 0.02),
        'cd_w_in': jnp.concatenate([nrm(ks[14], (N_ODD, D, CD_Q), D ** -0.5), nrm(ks[15], (N_ODD, D, CD_KV), D ** -0.5) * cd_kv_scale], -1),
        'cd_w_out': nrm(ks[16], (N_ODD, CD_OUT, D), CD_OUT ** -0.5 * BETA),
        'win_sink': nrm(ks[17], (N_ODD, WIN_HEADS), 0.5),
        'na_rpb': nrm(ks[18], (N_ODD, NA_HEADS, 2 * NA_ROWS_MAX - 1, 2 * NA_COLS - 1), 0.1),
        'moe_w_group': nrm(ks[19], (DEPTH, D, N_GROUPS), D ** -0.5),
        'moe_b_group': nrm(ks[20], (DEPTH, N_GROUPS), 0.01),
        'moe_w_router': nrm(ks[21], (DEPTH, D, N_EXPERTS), D ** -0.5),
        'moe_b_router': nrm(ks[22], (DEPTH, N_EXPERTS), 0.01),
        'moe_w1': nrm(ks[23], (DEPTH, N_EXPERTS, D, D_EXPERT), D ** -0.5),
        'moe_w3': nrm(ks[24], (DEPTH, N_EXPERTS, D, D_EXPERT), D ** -0.5),
        'moe_w2': nrm(ks[25], (DEPTH, N_EXPERTS, D_EXPERT, D), D_EXPERT ** -0.5 * BETA),
    }

def first_block(x, c, ctx, c_ctx, mod_w, mod_b, ln_g, ln_b, ab_w_in, ab_w_out, diff_lambda, diff_subln_g, gqa_qk_g, cd_w_in, cd_w_out, win_sink, na_rpb, moe_w_group, moe_b_group, moe_w_router, moe_b_router, moe_w1, moe_w3, moe_w2):
    b, s, d = x.shape
    n_ctx = ctx.shape[1]
    cos, sin = axial_rope_tables(s)
    silu_c = jax.nn.silu(c)
    silu_cc = jax.nn.silu(c_ctx)
    h_lat, h_ctx = x, ctx
    for i in range(DEPTH):
        last = i == DEPTH - 1
        j = i // 2
        mods = (silu_c @ mod_w[i] + mod_b[i]).reshape(b, 1, 6, d)
        n_cm = 2 if last else 6
        cmods = (silu_cc @ mod_w[i][:, :n_cm * d] + mod_b[i][:n_cm * d]).reshape(1, 1, n_cm, d)

        a_lat = modulate(h_lat, mods[:, :, 0], mods[:, :, 1])
        a_ctx = modulate(h_ctx, cmods[:, :, 0], cmods[:, :, 1])
        if i % 2 == 0:
            o_lat, o_ctx = mixer_ab(a_lat, a_ctx, last, ab_w_in[j], ab_w_out[j], diff_lambda[j], diff_subln_g[j], gqa_qk_g[j], lambda_init(i), cos, sin)
        else:
            o_lat, o_ctx = mixer_cd(a_lat, a_ctx, last, cd_w_in[j], cd_w_out[j], win_sink[j], na_rpb[j], cos, sin)
        h_lat = layer_norm(ALPHA * h_lat + mods[:, :, 2] * o_lat, ln_g[i, 0], ln_b[i, 0])

        def moe(tokens):
            return hier_moe(tokens, moe_w_group[i], moe_b_group[i], moe_w_router[i], moe_b_router[i], moe_w1[i], moe_w3[i], moe_w2[i])

        f_lat = modulate(h_lat, mods[:, :, 3], mods[:, :, 4]).reshape(b * s, d)
        if last:
            y_lat = moe(f_lat)
        else:
            h_ctx = layer_norm(ALPHA * h_ctx + cmods[:, :, 2] * o_ctx, ln_g[i, 0], ln_b[i, 0])
            f_ctx = modulate(h_ctx, cmods[:, :, 3], cmods[:, :, 4]).reshape(b * n_ctx, d)
            y = moe(jnp.concatenate([f_lat, f_ctx], 0))
            y_lat = y[:b * s]
            h_ctx = layer_norm(ALPHA * h_ctx + cmods[:, :, 5] * y[b * s:].reshape(b, n_ctx, d), ln_g[i, 1], ln_b[i, 1])
        h_lat = layer_norm(ALPHA * h_lat + mods[:, :, 5] * y_lat.reshape(b, s, d), ln_g[i, 1], ln_b[i, 1])
    return h_lat


ATTN_SCALE_2 = HEAD_DIM ** -0.5
SWA_HEADS = D_MODEL // 128
SWA_KV_HEADS = SWA_HEADS // 4
SWA_GROUP = SWA_HEADS // SWA_KV_HEADS
SWA_WINDOW = 128
SWA_BLOCK = 128
SC_WIDTH = D_MODEL // 2
SC_KSIZE = 3
MOBA_HEADS = D_MODEL // 128
MOBA_BLOCK = 256
MOBA_TOPK = 3
MOBA_QCHUNK = 32
N_ALIBI_HEADS = SWA_HEADS + MOBA_HEADS
FFN_HIDDEN = -(-8 * D_MODEL // (3 * 256)) * 256
ALPHA_2 = (2 * DEPTH) ** 0.25
BETA_2 = (8 * DEPTH) ** -0.25

A_Q = SWA_HEADS * HEAD_DIM
A_KV = SWA_KV_HEADS * HEAD_DIM
C_QKV = MOBA_HEADS * HEAD_DIM
PROJ_SIZES = (A_Q, A_KV, A_KV,
              SC_WIDTH, SC_WIDTH, SC_WIDTH,
              C_QKV, C_QKV, C_QKV,
              D_MODEL, D_MODEL, D_MODEL)
PROJ_SPLITS = tuple(int(s) for s in np.cumsum(PROJ_SIZES)[:-1])
PROJ_WIDTH = int(sum(PROJ_SIZES))


def alibi_slopes():
    i = jnp.arange(N_ALIBI_HEADS, dtype=jnp.float32)
    s = jnp.exp2(-8.0 * (i + 1.0) / N_ALIBI_HEADS)
    return s[:SWA_HEADS], s[SWA_HEADS:]

def layer_norm_2(x, g, b):
    xf = x.astype(jnp.float32)
    mu = jnp.mean(xf, axis=-1, keepdims=True)
    var = jnp.mean(jnp.square(xf - mu), axis=-1, keepdims=True)
    y = (xf - mu) * lax.rsqrt(var + LN_EPS) * g.astype(jnp.float32) + b.astype(jnp.float32)
    return y.astype(x.dtype)

def sliding_window_attention(q, k, v, sinks, slopes):
    B, S = q.shape[0], q.shape[1]
    nb = S // SWA_BLOCK
    qb = q.reshape(B, nb, SWA_BLOCK, SWA_KV_HEADS, SWA_GROUP, HEAD_DIM).astype(jnp.float32)
    kb = k.reshape(B, nb, SWA_BLOCK, SWA_KV_HEADS, HEAD_DIM)
    vb = v.reshape(B, nb, SWA_BLOCK, SWA_KV_HEADS, HEAD_DIM)
    shift = ((0, 0), (1, 0), (0, 0), (0, 0), (0, 0))
    kw = jnp.concatenate([jnp.pad(kb, shift)[:, :-1], kb], axis=2)
    vw = jnp.concatenate([jnp.pad(vb, shift)[:, :-1], vb], axis=2)
    logits = jnp.einsum('bnqhgd,bnkhd->bnhgqk', qb, kw.astype(jnp.float32)) * ATTN_SCALE_2
    blk = jnp.arange(nb)[:, None] * SWA_BLOCK
    qpos = blk + jnp.arange(SWA_BLOCK)[None, :]
    kpos = blk - SWA_BLOCK + jnp.arange(2 * SWA_BLOCK)[None, :]
    dist = qpos[:, :, None] - kpos[:, None, :]
    allowed = (dist >= 0) & (dist < SWA_WINDOW) & (kpos[:, None, :] >= 0)
    sl = slopes.reshape(SWA_KV_HEADS, SWA_GROUP)[:, :, None, None]
    logits = logits - sl * dist[:, None, None].astype(jnp.float32)
    logits = jnp.where(allowed[:, None, None], logits, -jnp.inf)
    sink = sinks.astype(jnp.float32).reshape(SWA_KV_HEADS, SWA_GROUP)[:, :, None, None]
    m = jnp.maximum(jnp.max(logits, axis=-1, keepdims=True), sink)
    p = jnp.exp(logits - m)
    denom = jnp.sum(p, axis=-1, keepdims=True) + jnp.exp(sink - m)
    out = jnp.einsum('bnhgqk,bnkhd->bnqhgd', p / denom, vw.astype(jnp.float32))
    return out.reshape(B, S, SWA_HEADS * HEAD_DIM).astype(q.dtype)

def gated_short_conv(h, gate_b, gate_c, conv_w):
    u = gate_c * h
    up = jnp.pad(u, ((0, 0), (SC_KSIZE - 1, 0), (0, 0)))
    S = h.shape[1]
    conv = up[:, 0:S] * conv_w[0] + up[:, 1:S + 1] * conv_w[1] + up[:, 2:S + 2] * conv_w[2]
    return gate_b * conv

def moba_attention(q, k, v, slopes):
    B, S = q.shape[0], q.shape[1]
    sp = -(-S // MOBA_BLOCK) * MOBA_BLOCK
    pad = ((0, 0), (0, sp - S), (0, 0), (0, 0))
    q, k, v = [jnp.pad(t, pad).transpose(0, 2, 1, 3) for t in (q, k, v)]
    nblk = sp // MOBA_BLOCK
    top = min(MOBA_TOPK, nblk)
    kbl = k.reshape(B, MOBA_HEADS, nblk, MOBA_BLOCK, HEAD_DIM)
    vbl = v.reshape(B, MOBA_HEADS, nblk, MOBA_BLOCK, HEAD_DIM)
    kmean = jnp.mean(kbl.astype(jnp.float32), axis=3)
    gate = jnp.einsum('bhsd,bhnd->bhsn', q.astype(jnp.float32), kmean)
    cur = jnp.arange(sp) // MOBA_BLOCK
    past = jnp.arange(nblk)[None, :] < cur[:, None]
    gate = jnp.where(past, gate, -jnp.inf)
    _, idx = lax.top_k(gate, top)
    nch = sp // MOBA_QCHUNK
    q_ch = q.reshape(B, MOBA_HEADS, nch, MOBA_QCHUNK, HEAD_DIM).transpose(2, 0, 1, 3, 4)
    idx_ch = idx.reshape(B, MOBA_HEADS, nch, MOBA_QCHUNK, top).transpose(2, 0, 1, 3, 4)
    bi = jnp.arange(B)[:, None, None, None]
    hi = jnp.arange(MOBA_HEADS)[None, :, None, None]
    sl4 = slopes[None, :, None, None]
    sl5 = slopes[None, :, None, None, None]
    koff = jnp.arange(MOBA_BLOCK)

    def chunk(args):
        c, qc, ic = args
        qpos = c * MOBA_QCHUNK + jnp.arange(MOBA_QCHUNK)
        own = (c * MOBA_QCHUNK) // MOBA_BLOCK
        qf = qc.astype(jnp.float32)
        kg = kbl[bi, hi, ic].astype(jnp.float32)
        vg = vbl[bi, hi, ic].astype(jnp.float32)
        ls = jnp.einsum('bhqd,bhqjkd->bhqjk', qf, kg) * ATTN_SCALE_2
        kpos_sel = ic[..., None] * MOBA_BLOCK + koff
        dist_sel = (qpos[None, None, :, None, None] - kpos_sel).astype(jnp.float32)
        valid = jnp.arange(top)[None, :] < (qpos // MOBA_BLOCK)[:, None]
        ls = jnp.where(valid[None, None, :, :, None], ls - sl5 * dist_sel, -jnp.inf)
        kown = lax.dynamic_index_in_dim(kbl, own, axis=2, keepdims=False).astype(jnp.float32)
        vown = lax.dynamic_index_in_dim(vbl, own, axis=2, keepdims=False).astype(jnp.float32)
        lo = jnp.einsum('bhqd,bhkd->bhqk', qf, kown) * ATTN_SCALE_2
        dist_own = qpos[:, None] - (own * MOBA_BLOCK + koff)[None, :]
        lo = jnp.where(dist_own >= 0, lo - sl4 * dist_own.astype(jnp.float32), -jnp.inf)
        logits = jnp.concatenate([ls.reshape(B, MOBA_HEADS, MOBA_QCHUNK, top * MOBA_BLOCK), lo], axis=-1)
        p = jax.nn.softmax(logits, axis=-1)
        ps = p[..., :top * MOBA_BLOCK].reshape(B, MOBA_HEADS, MOBA_QCHUNK, top, MOBA_BLOCK)
        po = p[..., top * MOBA_BLOCK:]
        return (jnp.einsum('bhqjk,bhqjkd->bhqd', ps, vg)
                + jnp.einsum('bhqk,bhkd->bhqd', po, vown))

    out = lax.map(chunk, (jnp.arange(nch), q_ch, idx_ch))
    out = out.transpose(1, 0, 3, 2, 4).reshape(B, sp, MOBA_HEADS * HEAD_DIM)[:, :S]
    return out.astype(q.dtype)

def hybrid_mixer(x, w_in, sinks, conv_w, w_br_a, w_br_b, w_br_c, w_out):
    B, S = x.shape[0], x.shape[1]
    proj = jnp.einsum('bsd,de->bse', x, w_in)
    a_q, a_k, a_v, b_h, b_b, b_c, c_q, c_k, c_v, g_a, g_b, g_c = jnp.split(proj, PROJ_SPLITS, axis=-1)
    slopes_a, slopes_c = alibi_slopes()
    y_a = sliding_window_attention(
        a_q.reshape(B, S, SWA_HEADS, HEAD_DIM),
        a_k.reshape(B, S, SWA_KV_HEADS, HEAD_DIM),
        a_v.reshape(B, S, SWA_KV_HEADS, HEAD_DIM), sinks, slopes_a)
    y_b = gated_short_conv(b_h, b_b, b_c, conv_w)
    y_c = moba_attention(
        c_q.reshape(B, S, MOBA_HEADS, HEAD_DIM),
        c_k.reshape(B, S, MOBA_HEADS, HEAD_DIM),
        c_v.reshape(B, S, MOBA_HEADS, HEAD_DIM), slopes_c)
    merged = (jax.nn.sigmoid(g_a) * (y_a @ w_br_a)
              + jax.nn.sigmoid(g_b) * (y_b @ w_br_b)
              + jax.nn.sigmoid(g_c) * (y_c @ w_br_c))
    return merged @ w_out

def swiglu(x, w_gate, w_up, w_down):
    return (jax.nn.silu(x @ w_gate) * (x @ w_up)) @ w_down

def second_inputs(seed: int = 0) -> dict:
    key = jax.random.key(seed)
    ks = jax.random.split(key, 16)
    f32 = jnp.float32
    nrm = lambda k, shape, s: jax.random.normal(k, shape, f32) * s
    L = DEPTH
    br_in = SWA_HEADS * HEAD_DIM
    return {
        'x': jax.random.normal(ks[0], (BATCH, SEQ, D_MODEL), f32),
        'w_in': nrm(ks[1], (L, D_MODEL, PROJ_WIDTH), D_MODEL ** -0.5),
        'attn_sinks': nrm(ks[2], (L, SWA_HEADS), 0.5),
        'conv_w': nrm(ks[3], (L, SC_KSIZE, SC_WIDTH), SC_KSIZE ** -0.5),
        'w_branch_a': nrm(ks[4], (L, br_in, D_MODEL), br_in ** -0.5 * BETA_2),
        'w_branch_b': nrm(ks[5], (L, SC_WIDTH, D_MODEL), SC_WIDTH ** -0.5 * BETA_2),
        'w_branch_c': nrm(ks[6], (L, MOBA_HEADS * HEAD_DIM, D_MODEL), (MOBA_HEADS * HEAD_DIM) ** -0.5 * BETA_2),
        'w_out': nrm(ks[7], (L, D_MODEL, D_MODEL), D_MODEL ** -0.5 * BETA_2),
        'ln1_g': 1.0 + nrm(ks[8], (L, D_MODEL), 0.02),
        'ln1_b': nrm(ks[9], (L, D_MODEL), 0.02),
        'w_ffn_gate': nrm(ks[10], (L, D_MODEL, FFN_HIDDEN), D_MODEL ** -0.5 * BETA_2),
        'w_ffn_up': nrm(ks[11], (L, D_MODEL, FFN_HIDDEN), D_MODEL ** -0.5 * BETA_2),
        'w_ffn_down': nrm(ks[12], (L, FFN_HIDDEN, D_MODEL), FFN_HIDDEN ** -0.5 * BETA_2),
        'ln2_g': 1.0 + nrm(ks[13], (L, D_MODEL), 0.02),
        'ln2_b': nrm(ks[14], (L, D_MODEL), 0.02),
    }

def second_block(x, w_in, attn_sinks, conv_w, w_branch_a, w_branch_b, w_branch_c, w_out,
              ln1_g, ln1_b, w_ffn_gate, w_ffn_up, w_ffn_down, ln2_g, ln2_b):
    for l in range(DEPTH):
        mix = hybrid_mixer(x, w_in[l], attn_sinks[l], conv_w[l], w_branch_a[l],
                           w_branch_b[l], w_branch_c[l], w_out[l])
        x = layer_norm_2(ALPHA_2 * x + mix, ln1_g[l], ln1_b[l])
        ffn = swiglu(x, w_ffn_gate[l], w_ffn_up[l], w_ffn_down[l])
        x = layer_norm_2(ALPHA_2 * x + ffn, ln2_g[l], ln2_b[l])
    return x


def setup_inputs(seed=0):
    out = dict(first_inputs(seed))
    for name, value in second_inputs(seed + 1).items():
        if name != "x":
            out[name + "_2"] = value
    return out


def reference(
    x, c, ctx, c_ctx, mod_w, mod_b, ln_g, ln_b, ab_w_in, ab_w_out, diff_lambda, diff_subln_g,
    gqa_qk_g, cd_w_in, cd_w_out, win_sink, na_rpb, moe_w_group, moe_b_group, moe_w_router,
    moe_b_router, moe_w1, moe_w3, moe_w2, w_in_2, attn_sinks_2, conv_w_2, w_branch_a_2,
    w_branch_b_2, w_branch_c_2, w_out_2, ln1_g_2, ln1_b_2, w_ffn_gate_2, w_ffn_up_2,
    w_ffn_down_2, ln2_g_2, ln2_b_2,
):
    x = first_block(
        x, c, ctx, c_ctx, mod_w, mod_b, ln_g, ln_b, ab_w_in, ab_w_out, diff_lambda,
        diff_subln_g, gqa_qk_g, cd_w_in, cd_w_out, win_sink, na_rpb, moe_w_group, moe_b_group,
        moe_w_router, moe_b_router, moe_w1, moe_w3, moe_w2,
    )
    return second_block(
        x, w_in_2, attn_sinks_2, conv_w_2, w_branch_a_2, w_branch_b_2, w_branch_c_2, w_out_2,
        ln1_g_2, ln1_b_2, w_ffn_gate_2, w_ffn_up_2, w_ffn_down_2, ln2_g_2, ln2_b_2,
    )


_drawn_inputs = setup_inputs


def setup_inputs(seed=0):
    import zlib

    import numpy as np

    out = dict(_drawn_inputs(seed))
    spreads = {}
    factors = {'mod_b': 5.454,
     'diff_lambda': 7.594,
     'diff_subln_g': 52.28,
     'gqa_qk_g': 63.425,
     'cd_w_out': 4.265,
     'win_sink': 40.815,
     'na_rpb': 51.881,
     'moe_b_group': 64.0,
     'moe_b_router': 54.472,
     'attn_sinks_2': 8.0}
    for name, (base, spread) in spreads.items():
        noise = np.random.default_rng([zlib.crc32(name.encode()), seed]).standard_normal(out[name].shape)
        drawn = base * np.exp(spread * noise) if base else spread * noise
        out[name] = jnp.asarray(drawn.astype(out[name].dtype))
    for name, factor in factors.items():
        out[name] = (out[name] * factor).astype(out[name].dtype)
    return out
```

```python
from contextlib import ExitStack

import numpy as np

import concourse.bass as bass
from concourse import mybir

ALU = mybir.AluOpType
ACT = mybir.ActivationFunctionType
AX = mybir.AxisListType
F32 = mybir.dt.float32
I32 = mybir.dt.int32
U32 = mybir.dt.uint32

P = 128
D = 1024
KC = D // P
TS = 256
HD = 64
DEPTH = 2
NE = 32
CAP = 128
FH = 512
RING = 6
NBLK = 40
NTAB = 48
FFN = 2816
FC = FFN // P
ALPHA = (2.0 * DEPTH) ** 0.25
SCALE = HD ** -0.5
NEG = -1e30
LAM_INIT = 0.2

CONSTS = {}


def build_consts():
    parts, at = [], 0

    def add(name, a):
        nonlocal at
        a = np.asarray(a, np.float32).reshape(P, -1)
        CONSTS[name] = (at, a.shape[1])
        parts.append(a)
        at += a.shape[1]

    p = np.arange(P)
    add("ident", np.eye(P))
    add("ones", np.ones((P, P)))
    add("mean_d", np.full((P, P), 1.0 / D))
    add("mean_p", np.full((P, P), 1.0 / P))
    add("mean_h", (p[:, None] // HD == p[None, :] // HD) / HD)
    add("before", p[:, None] < p[None, :])
    other = np.where(p % HD < HD // 2, p + HD // 2, p - HD // 2)
    add("swap", p[:, None] == other[None, :])
    t = np.arange(TS)
    inv = 10000.0 ** (-np.arange(HD // 4, dtype=np.float32) / np.float32(HD // 4))
    inv = inv.astype(np.float32)
    ang = np.concatenate([(t // 64).astype(np.float32)[:, None] * inv, (t % 64).astype(np.float32)[:, None] * inv], -1)
    cos, sin = np.cos(ang).T, np.sin(ang).T
    add("cos", np.tile(cos, (4, 1)))
    add("sin", np.concatenate([-sin, sin, -sin, sin], 0))
    q = (np.arange(2)[None, :] * P + p[:, None])[:, :, None]
    k = np.arange(TS)[None, None, :]
    add("near", np.where(np.abs(q - k) <= 128, 0.0, NEG))
    col0 = np.clip(q % 64 - 8, 0, 48)
    add("nbhd", np.where((k % 64 >= col0) & (k % 64 < col0 + 16), 0.0, NEG))
    add("swa", np.where((q - k >= 0) & (q - k < 128), k - q, NEG))
    add("causal", np.where(q - k >= 0, k - q, NEG))
    add("iota", np.tile(np.arange(NE), (P, 1)))
    add("jota", np.tile(np.arange(NTAB - NE), (P, 1)))
    add("token", np.arange(4)[None, :] * P + p[:, None])
    add("eps_ln", np.full((P, 1), 1e-5))
    add("eps_rms", np.full((P, 1), 1e-6))
    return np.ascontiguousarray(np.concatenate(parts, 1))


CONST_ARRAY = build_consts()


def program(nc, A, out):
    stack = ExitStack()
    with stack:
        def sb(name, shape, dt=F32):
            return stack.enter_context(nc.sbuf_tensor(name, shape, dt))

        sems = {}

        def sem(name):
            if name not in sems:
                sems[name] = stack.enter_context(nc.semaphore(name))
            return sems[name]

        def dram(name, shape, dt=F32):
            return nc.dram_tensor(name, shape, dt, kind="Internal").ap()

        ring = sb("ring", [P, RING, 4096])
        h = sb("h", [P, 2, KC, TS])
        a = sb("a", [P, 2, KC, TS])
        W = sb("W", [P, 15872])
        cst = sb("cst", [P, CONST_ARRAY.shape[1]])
        cc = sb("cc", [P, KC, 2])
        mods = sb("mods", [P, DEPTH, 6 * KC, 2])
        modb = sb("modb", [P, DEPTH, 6 * KC])
        lng = sb("lng", [P, 4, KC])
        lnb = sb("lnb", [P, 4, KC])
        lng2 = sb("lng2", [P, 4, KC])
        lnb2 = sb("lnb2", [P, 4, KC])
        subg = sb("subg", [P, 1])
        qkg = sb("qkg", [P, 2])
        sinks = sb("sinks", [P, 24])
        convw = sb("convw", [P, DEPTH, 3, 4])
        bgr = sb("bgr", [P, 36])
        neglam = sb("neglam", [P, 4])
        small = sb("small", [P, 64])
        w12 = sb("w12", [P, 2, 4])
        dest_i = sb("dest_i", [P, 2, 4], I32)
        gidx = sb("gidx", [P, 4, 8], U32)
        eidx = sb("eidx", [P, 4, 8], U32)
        tok_i = sb("tok_i", [P, NTAB], I32)
        gat = sb("gat", [P, 2], I32)
        tab_i = sb("tab_i", [1, NTAB], I32)
        np_i = sb("np_i", [1, 2], I32)
        PS = stack.enter_context(nc.psum_tensor("PS", [P, 8, 512], F32))

        Fd = dram("tokens_dram", [512, D])
        tokd = dram("slot_token_dram", [NTAB * CAP, 1])
        Yd = dram("slot_out_dram", [NBLK * CAP, D])
        Bd = dram("rpb_dram", [7, 8, 64, 64])

        def C(name):
            o, n = CONSTS[name]
            return cst[:, o:o + n]

        def CR(name, n):
            return C(name).rearrange("p (t k) -> p t k", t=n)

        ident = C("ident")

        def carve(at, *shape):
            n = int(np.prod(shape))
            v = W[:, at:at + n]
            names = "abcd"[:len(shape)]
            if len(shape) > 1:
                v = v.rearrange(f"p ({' '.join(names)}) -> p {' '.join(names)}",
                                **{names[i]: shape[i] for i in range(len(shape) - 1)})
            return v

        tiles = []

        def cols(name, w, n0, n=512):
            tiles.append((name, lambda r, n=n: r[:, 0:KC * n].rearrange("p (c n) -> p c n", c=KC),
                          w[:, n0:n0 + n].rearrange("(c p) n -> p c n", p=P)))

        def rows(name, w, k0, k=512):
            c = k // P
            tiles.append((name, lambda r, c=c: r[:, 0:c * D].rearrange("p (c n) -> p c n", c=c),
                          w[k0:k0 + k, :].rearrange("(c p) n -> p c n", p=P)))

        for l in range(DEPTH):
            for j in range(12):
                cols(f"mod{l}", A["mod_w"][l], 512 * j)
        seg_start = []
        for l in range(DEPTH):
            w_in, w_o = (A["ab_w_in"][0], A["ab_w_out"][0]) if l == 0 else (A["cd_w_in"][0], A["cd_w_out"][0])
            if l == 0:
                for n0, n in ((0, 512), (512, 512), (1024, 512), (1536, 512), (2048, 256)):
                    cols("in0", w_in, n0, n)
            else:
                for n0, n in ((0, 512), (512, 512), (1024, 256), (1280, 512), (1792, 512)):
                    cols("in1", w_in, n0, n)
            cols(f"out{l}", w_o, 0)
            cols(f"out{l}", w_o, 512)
            seg_start.append(len(tiles))
        for l in range(DEPTH):
            w = A["w_in_2"][l]
            for n0, n in ((0, 512), (512, 256), (768, 512), (1280, 512), (1792, 512),
                          (2304, 512), (2816, 512), (3328, 512)):
                cols(f"in2_{l}", w, n0, n)
            for b, br in enumerate("abc"):
                cols(f"gate2_{l}", w, 3840 + D * b)
                cols(f"gate2_{l}", w, 3840 + D * b + 512)
                rows(f"branch2_{l}", A[f"w_branch_{br}_2"][l], 0)
            cols(f"out2_{l}", A["w_out_2"][l], 0)
            cols(f"out2_{l}", A["w_out_2"][l], 512)
            for j in range(6):
                n = min(512, FFN - 512 * j)
                cols(f"ffn_gate_{l}", A["w_ffn_gate_2"][l], 512 * j, n)
                cols(f"ffn_up_{l}", A["w_ffn_up_2"][l], 512 * j, n)
            for j in range(6):
                rows(f"ffn_down_{l}", A["w_ffn_down_2"][l], 512 * j, min(512, FFN - 512 * j))
        SEG = [0, seg_start[0], seg_start[1], len(tiles)]

        def slot_of(seq):
            g = 0 if seq < SEG[1] else 1 if seq < SEG[2] else 2
            k = seq - SEG[g]
            return g, seq % RING, k // RING + 1, k

        def loaded(g, slot):
            return sem(f"tile_loaded_{g}_{slot}")

        def moe_loaded(l, slot):
            return sem(f"expert_tile_loaded_{l}_{slot}")

        used = []

        class Chain:

            def __init__(self, eng, name):
                self.eng, self.sem, self.n = eng, sem(name), 0

            def __call__(self, ins):
                self.n += 1
                ins.then_inc(self.sem, 1)
                self.eng.wait_ge(self.sem, self.n)

        stage_count = {}

        def end_stage(eng, name):
            stage_count[name] = stage_count.get(name, 0) + 1
            eng.drain().then_inc(sem("stage_ended"), 1)
            eng.wait_ge(sem("stage_ended"), 4 * stage_count[name])

        block = stack.enter_context(nc.Block())

        qT = carve(0, 8, 512)
        q1T = carve(0, 8, TS)
        rpbT = carve(2048, 2, 8, TS)
        kT = carve(6144, 6, 512)
        V = carve(9216, 4, 512)
        VS = carve(11264, 4, P)
        TMP = 11776
        sq_b = carve(TMP, 2, 512)
        rs_b = carve(TMP + 1024, 2, 512)
        rp_b = carve(TMP + 2048, 2, TS)
        kraw = carve(TMP + 2560, 512)
        oT = a[:, 0:2].rearrange("p s c t -> p (s c t)").rearrange("p (c t) -> p c t", c=KC)
        o1T = a[:, 0]

        def proj_list(l):
            L = []

            def feat(tile, m, dst, n, rms=None, rope=False):
                L.append(dict(tile=tile, kind="f", m=m, dst=dst, n=n, rms=rms, rope=rope))

            def toks(tile, c0, n, dst, nt=4):
                for t in range(nt):
                    L.append(dict(tile=tile, kind="t", c0=c0, n=n, tt=t, dst=dst[:, t, 0:n], rms=None, rope=False))

            if l == 0:
                for m in range(4):
                    feat(0, m, qT[:, m, :], 512, None, True)
                for m in range(4):
                    feat(1, m, qT[:, 4 + m, :], 512, 0, True)
                for m in range(4):
                    feat(2, m, kT[:, m, :], 512, None, True)
                toks(3, 0, 512, V)
                feat(4, 0, kraw, 512, 1, True)
                toks(4, P, P, VS)
            elif l == 1:
                for m in range(4):
                    feat(0, m, q1T[:, m, :], TS, None, True)
                for m in range(4):
                    feat(1, m, q1T[:, 4 + m, :], TS)
                feat(2, 0, kraw, 512, None, True)
                toks(2, P, P, VS)
                for m in range(4):
                    feat(3, m, kT[:, m, :], 512)
                toks(4, 0, 512, V)
            return L

        PROJ = [proj_list(0), proj_list(1)]

        qa2 = carve(0, 4, TS)
        qc2 = carve(1024, 4, TS)
        kc2 = carve(2048, 4, TS)
        kd2 = carve(3072, 2, TS)
        kraw2 = carve(3584, TS)
        va2 = carve(3840, 2, P)
        vc2 = carve(4096, 2, 512)
        bh2 = carve(5120, 4, TS)
        bb2 = carve(6144, 4, TS)
        bc2 = carve(7168, 4, TS)
        cv2 = carve(8192, 4, TS)
        ya2 = carve(9216, 4, TS)
        yc2 = carve(10240, 4, TS)
        G2 = carve(0, 8, TS)
        M2 = carve(2048, 8, TS)
        mt2 = carve(11776, 2, TS)
        hid2 = carve(0, FC, TS)
        sg2 = carve(6144, 4, TS)

        def proj2_list():
            L = []
            for t0, dst in ((0, qa2),):
                for m in range(4):
                    L.append(dict(tile=t0, kind="f", m=m, dst=dst[:, m, :], n=TS, rms=None, rope=False))
            L.append(dict(tile=1, kind="f", m=0, dst=kraw2, n=TS, rms=None, rope=False))
            for t in range(2):
                L.append(dict(tile=1, kind="t", c0=P, n=P, tt=t, dst=va2[:, t, :], rms=None, rope=False))
            for t0, dst in ((2, bh2), (3, bb2), (4, bc2), (5, qc2), (6, kc2)):
                for m in range(4):
                    L.append(dict(tile=t0, kind="f", m=m, dst=dst[:, m, :], n=TS, rms=None, rope=False))
            for t in range(2):
                L.append(dict(tile=7, kind="t", c0=0, n=512, tt=t, dst=vc2[:, t, :], rms=None, rope=False))
            return L

        PROJ2 = proj2_list()

        ATT = TMP

        def att_bufs(at):
            return dict(Sm=carve(at, 2, 512), Pm=carve(at + 1024, 4, 512)[:, :, :], PT=carve(at + 3072, 2, 512))

        def halves(k):
            return slice(HD * k, HD * k + HD)

        def units_of(stage):
            U = []
            if stage == "att0":
                for t in range(4):
                    k0 = 0 if t < 2 else TS
                    n = 512 - k0
                    for m in range(4):
                        U.append(dict(comps=[(qT[halves(i), m, t * P:t * P + P], kT[halves(i), m, k0:512]) for i in range(2)],
                                      n=n, mask=None, sink=None, diff=True, pb=0, dv=P,
                                      v=[V[:, k0 // P + kc, m * P:m * P + P] for kc in range(n // P)],
                                      out=oT[:, m, t * P:t * P + P]))
                    for hq in range(8):
                        i = hq % 2
                        kv = hq // 4
                        U.append(dict(comps=[(qT[halves(i), 4 + hq // 2, t * P:t * P + P], kT[halves(i), 4 + kv, k0:512])],
                                      n=n, mask=None, sink=None, diff=False, pb=HD * i, dv=HD,
                                      v=[VS[:, k0 // P + kc, kv * HD:kv * HD + HD] for kc in range(n // P)],
                                      out=oT[halves(i), 4 + hq // 2, t * P:t * P + P]))
            elif stage == "att1":
                for t in range(2):
                    for hq in range(8):
                        i, kv = hq % 2, hq // 4
                        U.append(dict(comps=[(q1T[halves(i), hq // 2, t * P:t * P + P], kT[halves(i), 4 + kv, :])],
                                      n=512, mask=(CR("near", 2)[:, t, :], TS, 1.0), sink=sinks[:, hq:hq + 1],
                                      diff=False, pb=HD * i, dv=HD,
                                      v=[VS[:, kc, kv * HD:kv * HD + HD] for kc in range(4)],
                                      out=o1T[halves(i), hq // 2, t * P:t * P + P]))
                    for hn in range(8):
                        i = hn % 2
                        U.append(dict(comps=[(q1T[halves(i), 4 + hn // 2, t * P:t * P + P], kT[halves(i), hn // 2, :])],
                                      n=512, mask=(rpbT[:, t, hn, :], TS, 1.0), sink=None,
                                      diff=False, pb=HD * i, dv=HD,
                                      v=[V[:, kc, hn * HD:hn * HD + HD] for kc in range(4)],
                                      out=o1T[halves(i), 4 + hn // 2, t * P:t * P + P]))
            else:
                l = int(stage[-1])
                slope = [2.0 ** (-8.0 * (i + 1.0) / 16) for i in range(16)]
                for t in range(2):
                    n = P * (t + 1)
                    for hq in range(8):
                        i, kv = hq % 2, hq // 4
                        U.append(dict(comps=[(qa2[halves(i), hq // 2, t * P:t * P + P], kd2[halves(i), kv, 0:n])],
                                      n=n, mask=(CR("swa", 2)[:, t, 0:n], n, slope[hq] / SCALE),
                                      sink=sinks[:, 8 + 8 * l + hq:9 + 8 * l + hq], diff=False, pb=HD * i, dv=HD,
                                      v=[va2[:, kc, kv * HD:kv * HD + HD] for kc in range(n // P)],
                                      out=ya2[halves(i), hq // 2, t * P:t * P + P]))
                    for hc in range(8):
                        i = hc % 2
                        U.append(dict(comps=[(qc2[halves(i), hc // 2, t * P:t * P + P], kc2[halves(i), hc // 2, 0:n])],
                                      n=n, mask=(CR("causal", 2)[:, t, 0:n], n, slope[8 + hc] / SCALE),
                                      sink=None, diff=False, pb=HD * i, dv=HD,
                                      v=[vc2[:, kc, hc * HD:hc * HD + HD] for kc in range(n // P)],
                                      out=yc2[halves(i), hc // 2, t * P:t * P + P]))
            j = 0
            for u in U:
                u["j0"] = j
                j += len(u["comps"])
                u["j1"] = j
            return U

        UNITS = {s: units_of(s) for s in ("att0", "att1", "att2_0", "att2_1")}
        comp_unit = {s: [u for u, x in enumerate(UNITS[s]) for _ in x["comps"]] for s in UNITS}

        def hv(T, c, buf=None):
            b = h if buf is None else buf
            return b[:, :, c, :] if T == 512 else b[:, 0, c, :]

        X = dict(xg=carve(0, 2, D), xe=carve(2048, 2, KC, P), hid=carve(4096, 512), sil=carve(4608, 512),
                 hidT=carve(5120, 4, P), ysb=carve(5632, 2, D), y1=carve(7680, 2, D), y2=carve(9728, 2, D),
                 rows=carve(7680, 2, D), tz=carve(11776, 2, 512))
        rb = 12800
        R = {}
        for name, shape in (("L", (4, 36)), ("g8", (4, 8)), ("gmx", (4, 8)), ("ohg", (4, 4)), ("ge", (4, 4)),
                            ("em", (4, 32)), ("emx", (4, 8)), ("A1", (4, 32)), ("A2", (4, 32)), ("AB", (4, 32)),
                            ("tmp", (4, 32)), ("f", (16, 4)), ("ovf", (32,)), ("cum", (48,)), ("cum2", (48,)),
                            ("ob", (32,)), ("jt", (16, 32)), ("tabf", (48,)), ("wgr", (KC, 36))):
            R[name] = carve(rb, *shape)
            rb += int(np.prod(shape))
        R["A"] = [R["A1"], R["A2"], R["AB"]]
        R["tokrow"] = W[0:NTAB, rb:rb + P]
        R["zero"] = W[0:NTAB, rb + P:rb + 2 * P]
        rb += 2 * P
        assert rb <= 15872, rb
        wgr = R["wgr"]

        def proj_total(L):
            nr, np_ = sum(e["rms"] is not None for e in L), sum(e["rope"] for e in L)
            return dict(mm=len(L), evacuated=len(L), squared=nr, stat=nr, root=nr, normed=nr, rotated=np_, roped=np_)

        def att_total(s):
            u, j = len(UNITS[s]), len(comp_unit[s])
            return dict(scores=j, max=j, exp=j, probs=u, transposed=u, turned=u, pv=u, out=u)

        NORM = dict(mean=1, squared=KC, var=KC, std=1, centred=KC, scaled=KC, normed=KC)
        MIX = dict(NORM, mm=KC, gated=KC, z=KC)
        FAMILIES = {
            "projection": [("proj0", proj_total(PROJ[0])), ("proj1", proj_total(PROJ[1])),
                           ("proj2_0", proj_total(PROJ2)), ("proj2_1", proj_total(PROJ2))],
            "attention": [(s, att_total(s)) for s in ("att0", "att1", "att2_0", "att2_1")],
            "norm": [("mix0", MIX), ("moe0", dict(NORM, mm=0, gated=0, z=8)), ("mix1", MIX),
                     ("moe1", dict(NORM, mm=0, gated=0, z=4)),
                     ("mix2_0", dict(MIX, gated=0)), ("down_0", dict(NORM, mm=0, gated=0, z=KC)),
                     ("mix2_1", dict(MIX, gated=0)), ("down_1", dict(NORM, mm=0, gated=0, z=KC))],
            "branch": [(f"branch_{l}", dict(mm=48, gates=24, merged=24)) for l in range(DEPTH)],
            "ffn": [(f"ffn_{l}", dict(mm=2 * FC, silu=FC, hid=FC)) for l in range(DEPTH)],
        }
        family = {tag: f for f, L in FAMILIES.items() for tag, _ in L}

        def sig(tag, what):
            return sem(f"{family[tag]}_{what}")

        def at(tag, what, v):
            base = 0
            for t, totals in FAMILIES[family[tag]]:
                if t == tag:
                    return sig(tag, what), base + v
                base += totals[what]

        @block.tensor
        def _(pe):
            taken = [0]

            def take(name):
                seq = taken[0]
                assert tiles[seq][0] == name, (tiles[seq][0], name)
                assert len(used) == seq
                g, slot, n, _ = slot_of(seq)
                pe.wait_ge(loaded(g, slot), 16 * n)
                taken[0] += 1
                return tiles[seq][1](ring[:, slot, :])

            def release(s, v):
                used.append((s, v))

            pe.wait_ge(sem("silu_c"), 1)
            for l in range(DEPTH):
                for j in range(12):
                    w = take(f"mod{l}")
                    for m in range(4):
                        for c in range(KC):
                            mm = pe.matmul(PS[:, l, (4 * j + m) * 2:(4 * j + m) * 2 + 2], w[:, c, m * P:m * P + P],
                                           cc[:, c, :], start=(c == 0), stop=(c == KC - 1))
                    mm.then_inc(sem("mods_mm"), 1)
                    release(sem("mods_mm"), 12 * l + j + 1)
            end_stage(pe, "pe")

            def project(tag, L, tile_name, x, wide):
                n_rms = n_rope = 0
                w, cur = None, -1

                def stats(g):
                    nonlocal n_rms
                    if g >= 0 and L[g]["rms"] is not None:
                        pe.wait_ge(*at(tag, "squared", n_rms + 1))
                        if n_rms >= 2:
                            pe.wait_ge(*at(tag, "root", n_rms - 1))
                        pe.matmul(PS[:, 4 + n_rms % 2, 0:512], C("mean_h"), sq_b[:, n_rms % 2, :],
                                  start=True, stop=True).then_inc(sig(tag, "stat"), 1)
                        n_rms += 1

                def rotate(g):
                    nonlocal n_rope
                    if g >= 0 and L[g]["rope"]:
                        pe.wait_ge(*at(tag, "evacuated", g + 1))
                        if L[g]["rms"] is not None:
                            pe.wait_ge(*at(tag, "normed", sum(x["rms"] is not None for x in L[:g + 1])))
                        if n_rope >= 2:
                            pe.wait_ge(*at(tag, "roped", n_rope - 1))
                        pe.matmul(PS[:, 6 + n_rope % 2, 0:TS], C("swap"), L[g]["dst"][:, 0:TS],
                                  start=True, stop=True).then_inc(sig(tag, "rotated"), 1)
                        n_rope += 1

                for g, e in enumerate(L):
                    if e["tile"] != cur:
                        w, cur = take(tile_name), e["tile"]
                    if g >= 4:
                        pe.wait_ge(*at(tag, "evacuated", g - 3))
                    for c in range(KC):
                        if e["kind"] == "f":
                            T = e["n"]
                            o = PS[:, g % 4, 0:T]
                            rhs = x[:, :, c, :] if T == 512 else x[:, 0, c, :]
                            if T == 512:
                                o = o.rearrange("p (s t) -> p s t", s=2)
                            mm = pe.matmul(o, w[:, c, e["m"] * P:e["m"] * P + P], rhs,
                                           start=(c == 0), stop=(c == KC - 1))
                        else:
                            tt = e["tt"]
                            mm = pe.matmul(PS[:, g % 4, 0:e["n"]], x[:, tt // 2, c, (tt % 2) * P:(tt % 2) * P + P],
                                           w[:, c, e["c0"]:e["c0"] + e["n"]], start=(c == 0), stop=(c == KC - 1))
                    mm.then_inc(sig(tag, "mm"), 1)
                    if g + 1 == len(L) or L[g + 1]["tile"] != cur:
                        release(*at(tag, "mm", g + 1))
                    stats(g - 1)
                    rotate(g - 2)
                stats(len(L) - 1)
                rotate(len(L) - 2)
                rotate(len(L) - 1)
                end_stage(pe, "pe")

            def attention(stage):
                U, cu = UNITS[stage], comp_unit[stage]
                for i in range(len(U) + 3):
                    if i < len(U):
                        u = U[i]
                        for k, (q, kk) in enumerate(u["comps"]):
                            j = u["j0"] + k
                            if j >= 4:
                                pe.wait_ge(*at(stage, "exp", j - 3))
                            pe.matmul(PS[:, j % 4, 0:u["n"]], q, kk, start=True, stop=True)\
                              .then_inc(sig(stage, "scores"), 1)
                    if 0 <= i - 2 < len(U):
                        v = i - 2
                        u = U[v]
                        pe.wait_ge(*at(stage, "probs", v + 1))
                        if v >= 2:
                            pe.wait_ge(*at(stage, "turned", v - 1))
                        for kc in range(u["n"] // P):
                            mm = pe.transpose(PS[:, 4 + v % 2, kc * P:kc * P + P],
                                              UB["Pm"][:, u["j0"] % 4, kc * P:kc * P + P], ident)
                        mm.then_inc(sig(stage, "transposed"), 1)
                    if 0 <= i - 3 < len(U):
                        v = i - 3
                        u = U[v]
                        pe.wait_ge(*at(stage, "turned", v + 1))
                        if v >= 2:
                            pe.wait_ge(*at(stage, "out", v - 1))
                        nk = u["n"] // P
                        for kc in range(nk):
                            mm = pe.matmul(PS[u["pb"]:u["pb"] + u["dv"], 6 + v % 2, 0:P], u["v"][kc],
                                           UB["PT"][:, v % 2, kc * P:kc * P + P], start=(kc == 0), stop=(kc == nk - 1))
                        mm.then_inc(sig(stage, "pv"), 1)
                end_stage(pe, "pe")

            UB = att_bufs(ATT)

            def subln():
                for m in range(4):
                    pe.wait_ge(sem("subln_squared"), m + 1)
                    pe.matmul(PS[:, m, :], C("mean_p"), carve(m * 512, 512), start=True, stop=True)\
                      .then_inc(sem("subln_stat"), 1)
                end_stage(pe, "pe")

            def out_proj(tag, tile_name, T, x):
                for g in range(KC):
                    if g % 4 == 0:
                        w = take(tile_name)
                    for c in range(KC):
                        mm = pe.matmul(PS[:, g, 0:T], w[:, c, (g % 4) * P:(g % 4) * P + P], x[:, c, 0:T],
                                       start=(c == 0), stop=(c == KC - 1))
                    mm.then_inc(sig(tag, "mm"), 1)
                    if g % 4 == 3:
                        release(*at(tag, "mm", g + 1))

            def norm(tag, T, per_chunk):
                for c in range(KC):
                    pe.wait_ge(*at(tag, "z", per_chunk(c)))
                    if c == 0:
                        pe.wait_ge(*at(tag, "z", per_chunk(c + 7)))
                    o = PS[:, 0, 0:T].rearrange("p (s t) -> p s t", s=2) if T == 512 else PS[:, 0, 0:T]
                    mm = pe.matmul(o, C("mean_d"), hv(T, c), start=(c == 0), stop=(c == KC - 1))
                mm.then_inc(sig(tag, "mean"), 1)
                for c in range(KC):
                    pe.wait_ge(*at(tag, "squared", c + 1))
                    mm = pe.matmul(PS[:, 1, 0:T], C("mean_d"), carve(14848 + (c % 2) * 512, T),
                                   start=(c == 0), stop=(c == KC - 1))
                    mm.then_inc(sig(tag, "var"), 1)
                end_stage(pe, "pe")

            def moe(l):
                T = 512 if l == 0 else TS
                nt = T // P
                pe.wait_ge(sem("router_weights"), 48 * (l + 1))
                for tt in range(nt):
                    for c in range(KC):
                        mm = pe.matmul(PS[:, 0, tt * 36:tt * 36 + 36], a[:, tt // 2, c, (tt % 2) * P:(tt % 2) * P + P],
                                       wgr[:, c, :], start=(c == 0), stop=(c == KC - 1))
                mm.then_inc(sem("logits"), 1)
                for tt in range(nt):
                    for hf in range(2):
                        k = 2 * tt + hf
                        if k >= 4:
                            pe.wait_ge(sem(f"rows{l}_copied"), k - 3)
                        for c in range(4):
                            mm = pe.transpose(PS[:, 4 + k % 4, c * P:c * P + P],
                                              a[:, tt // 2, 4 * hf + c, (tt % 2) * P:(tt % 2) * P + P], ident)
                        mm.then_inc(sem(f"rows{l}"), 1)
                pe.wait_ge(sem("chosen"), l + 1)
                both = R["A"][2]
                for tt in range(nt):
                    for t2 in range(tt + 1):
                        pe.matmul(PS[:, 1, tt * NE:tt * NE + NE], C("before") if t2 == tt else C("ones"), both[:, t2, :],
                                  start=(t2 == 0), stop=(t2 == tt))
                for t2 in range(nt):
                    mm = pe.matmul(PS[:, 2, 0:NE], C("ones"), both[:, t2, :], start=(t2 == 0), stop=(t2 == nt - 1))
                mm.then_inc(sem("ranks"), 1)
                pe.wait_ge(sem(f"slots_back{l}"), 16)
                pe.transpose(PS[:, 3, 0:NTAB], R["tokrow"], ident[0:NTAB, 0:NTAB]).then_inc(sem("slots_turned"), 1)

                pe.wait_ge(sem(f"routed{l}"), 2)
                pairs = pe.value_load(np_i[0:1, 0:1], min_val=NE // 2, max_val=20)
                r0 = SEG[l + 1] % RING

                def turn_in(b1, count):
                    pe.wait_ge(sem(f"gathered{l}_{b1}"), count)
                    for c in range(KC):
                        mm = pe.transpose(PS[:, c // 4, (c % 4) * P:(c % 4) * P + P],
                                          X["xg"][:, b1, c * P:c * P + P], ident)
                    mm.then_inc(sem(f"x_turned{l}"), 1)

                turn_in(0, 16)
                with pe.Fori(0, pairs) as i:
                    for s in range(2):
                        w1 = ring[:, (r0 + 3 * s) % RING, :].rearrange("p (c n) -> p c n", c=KC)
                        w3 = ring[:, (r0 + 3 * s + 1) % RING, :].rearrange("p (c n) -> p c n", c=KC)
                        w2 = ring[:, (r0 + 3 * s + 2) % RING, :].rearrange("p (c n) -> p c n", c=4)
                        pe.wait_ge(sem(f"x_ready{l}"), i * 2 + (s + 1))
                        pe.wait_ge(moe_loaded(l, (r0 + 3 * s) % RING), i * 16 + 16)
                        for c in range(KC):
                            mm = pe.matmul(PS[:, 2, :], X["xe"][:, s, c, :], w1[:, c, :], start=(c == 0), stop=(c == KC - 1))
                        mm.then_inc(sem(f"w1_done{l}"), 1)
                        pe.wait_ge(moe_loaded(l, (r0 + 3 * s + 1) % RING), i * 16 + 16)
                        for c in range(KC):
                            mm = pe.matmul(PS[:, 3, :], X["xe"][:, s, c, :], w3[:, c, :], start=(c == 0), stop=(c == KC - 1))
                        mm.then_inc(sem(f"w3_done{l}"), 1)
                        turn_in(1 - s, i * 16 + 16 * (s + 1))
                        pe.wait_ge(sem(f"hidden{l}"), i * 2 + (s + 1))
                        for c in range(4):
                            mm = pe.transpose(PS[:, 4, c * P:c * P + P], X["hid"][:, c * P:c * P + P], ident)
                        mm.then_inc(sem(f"hidden_turned{l}"), 1)
                        pe.wait_ge(sem(f"hidden_ready{l}"), i * 2 + (s + 1))
                        pe.wait_ge(sem(f"y_copied{l}"), i * 4 + (2 * s + 2))
                        pe.wait_ge(moe_loaded(l, (r0 + 3 * s + 2) % RING), i * 16 + 16)
                        for n in range(2):
                            for c in range(4):
                                mm = pe.matmul(PS[:, 6 + n, :], X["hidT"][:, c, :], w2[:, c, n * 512:n * 512 + 512],
                                               start=(c == 0), stop=(c == 3))
                        mm.then_inc(sem(f"w2_done{l}"), 1)
                end_stage(pe, "pe")
                for tt in range(nt):
                    pe.wait_ge(sem(f"mixed{l}"), tt + 1)
                    for hf in range(2):
                        k = 2 * tt + hf
                        if k >= 4:
                            pe.wait_ge(*at(f"moe{l}", "z", k - 3))
                        for c in range(4):
                            mm = pe.transpose(PS[:, 2 + k % 4, c * P:c * P + P],
                                              X["y1"][:, tt % 2, (4 * hf + c) * P:(4 * hf + c) * P + P], ident)
                        mm.then_inc(sem(f"moe{l}_back"), 1)
                norm(f"moe{l}", T, lambda c: 2 * nt)

            project("proj0", PROJ[0], "in0", a, True)
            attention("att0")
            subln()
            out_proj("mix0", "out0", 512, oT)
            norm("mix0", 512, lambda c: KC)
            moe(0)
            project("proj1", PROJ[1], "in1", a, True)
            attention("att1")
            out_proj("mix1", "out1", TS, o1T)
            norm("mix1", TS, lambda c: KC)
            moe(1)
            for l in range(DEPTH):
                project(f"proj2_{l}", PROJ2, f"in2_{l}", h, False)
                attention(f"att2_{l}")
                tag = f"branch_{l}"
                for b, y in enumerate((ya2, cv2, yc2)):
                    for part in range(2):
                        for m in range(KC):
                            if part == 0 and m % 4 == 0:
                                w = take(f"gate2_{l}")
                            if part == 1 and m == 0:
                                w = take(f"branch2_{l}")
                            g = (2 * b + part) * KC + m
                            if part == 0 and b:
                                pe.wait_ge(*at(tag, "merged", (b - 1) * KC + m + 1))
                            if part == 1:
                                pe.wait_ge(*at(tag, "gates", b * KC + m + 1))
                            n = KC if part == 0 else 4
                            for c in range(n):
                                lhs = w[:, c, (m % 4) * P:(m % 4) * P + P] if part == 0 else w[:, c, m * P:m * P + P]
                                rhs = h[:, 0, c, :] if part == 0 else y[:, c, :]
                                mm = pe.matmul(PS[:, m, 0:TS], lhs, rhs, start=(c == 0), stop=(c == n - 1))
                            mm.then_inc(sig(tag, "mm"), 1)
                            if (part == 0 and m % 4 == 3) or (part == 1 and m == 7):
                                release(*at(tag, "mm", g + 1))
                end_stage(pe, "pe")
                out_proj(f"mix2_{l}", f"out2_{l}", TS, M2)
                norm(f"mix2_{l}", TS, lambda c: KC)
                tag = f"ffn_{l}"
                g = 0
                for j in range(6):
                    nm = min(4, FC - 4 * j)
                    for part, nm_ in ((0, f"ffn_gate_{l}"), (1, f"ffn_up_{l}")):
                        w = take(nm_)
                        for m in range(nm):
                            k = 4 * j + m
                            if j and part == 0:
                                pe.wait_ge(*at(tag, "silu", k - 3))
                            if j and part == 1:
                                pe.wait_ge(*at(tag, "hid", k - 3))
                            for c in range(KC):
                                mm = pe.matmul(PS[:, 4 * part + m, 0:TS], w[:, c, m * P:m * P + P], h[:, 0, c, :],
                                               start=(c == 0), stop=(c == KC - 1))
                            mm.then_inc(sig(tag, "mm"), 1)
                            g += 1
                        release(*at(tag, "mm", g))
                end_stage(pe, "pe")
                for j in range(6):
                    nk = min(4, FC - 4 * j)
                    w = take(f"ffn_down_{l}")
                    for c in range(nk):
                        for m in range(KC):
                            mm = pe.matmul(PS[:, m, 0:TS], w[:, c, m * P:m * P + P], hid2[:, 4 * j + c, :],
                                           start=(j == 0 and c == 0), stop=(4 * j + c == FC - 1))
                    mm.then_inc(sem(f"down_{l}"), 1)
                    release(sem(f"down_{l}"), j + 1)
                norm(f"down_{l}", TS, lambda c: KC)
            assert taken[0] == len(tiles)

        @block.scalar
        def _(act):
            link = Chain(act, "act_link")
            loads = [(cst[:, :], A["consts"]), (small[:, 0:16], A["cT"]), (h[:, 0], A["xT"]), (h[:, 1], A["ctxT"]),
                     (modb[:, :, :], A["mod_bT"]), (lng[:, :, :], A["ln_gT"]), (lnb[:, :, :], A["ln_bT"]),
                     (lng2[:, :, :], A["ln_g2T"]), (lnb2[:, :, :], A["ln_b2T"]), (subg[:, :], A["sublnT"]),
                     (qkg[0:HD, :], A["qkgT"]), (qkg[HD:P, :], A["qkgT"]),
                     (sinks[:, 0:8], A["win_sink"].to_broadcast([P, 8])),
                     (sinks[:, 8:24], A["attn_sinks"].to_broadcast([P, 16])),
                     (convw[:, :, :, :], A["convT"]), (carve(0, 256), A["diff_lambda"].to_broadcast([P, 256]))]
            for o, i in loads:
                act.dma_start(o, i).then_inc(sem("params"), 16)
            for dr in range(7):
                act.dma_start(Bd[dr], bass.AP(A["na_rpb"].tensor, (dr + 4) * 31 + 15, [[465, 8], [-1, 64], [1, 64]]))\
                   .then_inc(sem("rpb_spread"), 16)
            act.wait_ge(sem("params"), 16 * len(loads))
            act.activation(cc[:, :, :], small[:, 0:16].rearrange("p (c s) -> p c s", s=2), ACT.Silu)\
               .then_inc(sem("silu_c"), 1)
            act.wait_ge(sem("lam_dot"), 1)
            act.activation(neglam[:, 1:3], neglam[:, 1:3], ACT.Exp).then_inc(sem("lam_exp"), 1)
            end_stage(act, "act")

            def project(tag, L, dup, rpb=False):
                if rpb:
                    act.wait_ge(sem("rpb_spread"), 16 * 7)
                    for t in range(2):
                        for r in range(2):
                            for kr in range(4):
                                act.dma_start(rpbT[64 * r:64 * r + 64, t, :, 64 * kr:64 * kr + 64],
                                              Bd[kr - (2 * t + r) + 3].rearrange("h q k -> q h k"))\
                                   .then_inc(sem("rpb_loaded"), 16)
                n_rms = 0

                def root(g):
                    nonlocal n_rms
                    if g >= 0 and L[g]["rms"] is not None:
                        act.wait_ge(*at(tag, "stat", n_rms + 1))
                        if n_rms >= 2:
                            act.wait_ge(*at(tag, "normed", n_rms - 1))
                        act.activation(rs_b[:, n_rms % 2, :], PS[:, 4 + n_rms % 2, :], ACT.Sqrt, bias=C("eps_rms"))\
                           .then_inc(sig(tag, "root"), 1)
                        n_rms += 1

                n_sq = 0
                for g, e in enumerate(L):
                    act.wait_ge(*at(tag, "mm", g + 1))
                    act.activation(e["dst"], PS[:, g % 4, 0:e["n"]], ACT.Copy).then_inc(sig(tag, "evacuated"), 1)
                    if e["rms"] is not None:
                        if n_sq >= 2:
                            act.wait_ge(*at(tag, "stat", n_sq - 1))
                        act.wait_ge(*at(tag, "evacuated", g + 1))
                        act.activation(sq_b[:, n_sq % 2, :], e["dst"], ACT.Square).then_inc(sig(tag, "squared"), 1)
                        n_sq += 1
                    root(g - 1)
                root(len(L) - 1)
                kr, kd, n = dup
                nr = sum(e["rope"] for e in L)
                if nr:
                    act.wait_ge(*at(tag, "roped", nr))
                else:
                    act.wait_ge(*at(tag, "evacuated", len(L)))
                for kv in range(2):
                    for i in range(2):
                        act.activation(kd[halves(i), kv, 0:n], kr[halves(kv), 0:n], ACT.Copy)
                end_stage(act, "act")

            def attention(stage):
                U, cu = UNITS[stage], comp_unit[stage]
                B = att_bufs(ATT)
                for i in range(len(U) + 3):
                    if i < len(U):
                        u = U[i]
                        for j in range(u["j0"], u["j1"]):
                            act.wait_ge(*at(stage, "max", j + 1))
                            if j >= 4:
                                act.wait_ge(*at(stage, "transposed", cu[j - 4] + 1))
                            src = B["Sm"][:, j % 2, 0:u["n"]] if u["mask"] else PS[:, j % 4, 0:u["n"]]
                            if u["sink"] is not None:
                                act.activation(small[:, 24 + j % 8:25 + j % 8], u["sink"], ACT.Exp,
                                               bias=small[:, 8 + j % 8:9 + j % 8])
                            act.activation(B["Pm"][:, j % 4, 0:u["n"]], src, ACT.Exp, bias=small[:, 8 + j % 8:9 + j % 8],
                                           scale=SCALE, accum_out=small[:, 16 + j % 8:17 + j % 8])\
                               .then_inc(sig(stage, "exp"), 1)
                    if 0 <= i - 2 < len(U):
                        v = i - 2
                        act.wait_ge(*at(stage, "transposed", v + 1))
                        if v >= 2:
                            act.wait_ge(*at(stage, "pv", v - 1))
                        act.activation(B["PT"][:, v % 2, 0:U[v]["n"]], PS[:, 4 + v % 2, 0:U[v]["n"]], ACT.Copy)\
                           .then_inc(sig(stage, "turned"), 1)
                    if 0 <= i - 3 < len(U):
                        v = i - 3
                        u = U[v]
                        act.wait_ge(*at(stage, "pv", v + 1))
                        act.activation(u["out"], PS[u["pb"]:u["pb"] + u["dv"], 6 + v % 2, 0:P], ACT.Copy)\
                           .then_inc(sig(stage, "out"), 1)
                end_stage(act, "act")

            def subln():
                for m in range(4):
                    act.activation(carve(m * 512, 512), oT[:, m, :], ACT.Square).then_inc(sem("subln_squared"), 1)
                for m in range(4):
                    act.wait_ge(sem("subln_stat"), m + 1)
                    act.activation(carve(2048 + m * 512, 512), PS[:, m, :], ACT.Sqrt, bias=C("eps_rms"))\
                       .then_inc(sem("subln_root"), 1)
                end_stage(act, "act")

            def gated(tag, l, T):
                for g in range(KC):
                    act.wait_ge(*at(tag, "mm", g + 1))
                    if g >= 2:
                        act.wait_ge(*at(tag, "z", g - 1))
                    for s in range(T // TS):
                        ins = act.activation(carve(13824 + (g % 2) * 512 + s * TS, TS), PS[:, g, s * TS:s * TS + TS],
                                             ACT.Copy, scale=mods[:, l, 2 * KC + g, s:s + 1])
                    ins.then_inc(sig(tag, "gated"), 1)

            def norm(tag, T, gain, bias, extra=None):
                for c in range(KC):
                    act.wait_ge(*at(tag, "centred", c + 1))
                    if c >= 2:
                        act.wait_ge(*at(tag, "var", c - 1))
                    o = carve(14848 + (c % 2) * 512, T)
                    if T == 512:
                        o = o.rearrange("p (s t) -> p s t", s=2)
                    act.activation(o, hv(T, c), ACT.Square).then_inc(sig(tag, "squared"), 1)
                act.wait_ge(*at(tag, "var", KC))
                act.wait_ge(*at(tag, "squared", KC))
                act.activation(carve(14848, T), PS[:, 1, 0:T], ACT.Sqrt, bias=C("eps_ln")).then_inc(sig(tag, "std"), 1)
                for c in range(KC):
                    act.wait_ge(*at(tag, "scaled", c + 1))
                    act.activation(hv(T, c), hv(T, c), ACT.Identity, scale=gain[:, c:c + 1], bias=bias[:, c:c + 1])\
                       .then_inc(sig(tag, "normed"), 1)
                end_stage(act, "act")

            def moe(l):
                T = 512 if l == 0 else TS
                nt = T // P
                act.dma_start(wgr[:, :, 0:4], A["wgT"][:, l]).then_inc(sem("router_weights"), 16)
                act.dma_start(wgr[:, :, 4:36], A["wrT"][:, l]).then_inc(sem("router_weights"), 16)
                act.dma_start(bgr[:, :], A["bgr"][l:l + 1, :].to_broadcast([P, 36])).then_inc(sem("router_weights"), 16)
                for tt in range(nt):
                    for hf in range(2):
                        k = 2 * tt + hf
                        act.wait_ge(sem(f"rows{l}"), k + 1)
                        if tt >= 2 and hf == 0:
                            act.wait_ge(sem(f"rows{l}_stored_{tt % 2}"), 16)
                        act.activation(X["rows"][:, tt % 2, hf * 512:hf * 512 + 512], PS[:, 4 + k % 4, :], ACT.Copy)\
                           .then_inc(sem(f"rows{l}_copied"), 1)
                    act.wait_ge(sem(f"rows{l}_copied"), 2 * tt + 2)
                    act.dma_start(Fd[tt * P:tt * P + P, :], X["rows"][:, tt % 2, :]).then_inc(sem(f"rows{l}_stored_{tt % 2}"), 16)
                act.wait_ge(sem("group_max"), l + 1)
                act.activation(R["ge"][:, 0:nt, :], R["ge"][:, 0:nt, :], ACT.Exp).then_inc(sem("group_exp"), 1)
                act.wait_ge(sem("pair_diff"), l + 1)
                act.activation(R["f"][:, 2, 0:nt], R["f"][:, 2, 0:nt], ACT.Exp).then_inc(sem("pair_exp"), 1)

                act.wait_ge(sem(f"routed{l}"), 2)
                pairs = act.value_load(np_i[0:1, 0:1], min_val=NE // 2, max_val=20)

                def tokens_in(b1, count):
                    act.wait_ge(sem(f"x_turned{l}"), count)
                    act.activation(X["xe"][:, b1, 0:4, :], PS[:, 0, :].rearrange("p (c t) -> p c t", c=4), ACT.Copy)
                    act.activation(X["xe"][:, b1, 4:8, :], PS[:, 1, :].rearrange("p (c t) -> p c t", c=4), ACT.Copy)\
                       .then_inc(sem(f"x_ready{l}"), 1)

                tokens_in(0, 2)
                with act.Fori(0, pairs) as i:
                    for s in range(2):
                        act.wait_ge(sem(f"w1_done{l}"), i * 2 + (s + 1))
                        act.activation(X["sil"], PS[:, 2, :], ACT.Silu).then_inc(sem(f"silu{l}"), 1)
                        act.wait_ge(sem(f"w3_done{l}"), i * 2 + (s + 1))
                        tokens_in(1 - s, i * 2 + (s + 3))
                        act.wait_ge(sem(f"w2_done{l}"), i * 2 + (s + 1))
                        act.wait_ge(sem(f"y_stored{l}_{s}"), i * 16 + 16)
                        act.activation(X["ysb"][:, s, 0:512], PS[:, 6, :], ACT.Copy).then_inc(sem(f"y_copied{l}"), 1)
                        act.wait_ge(sem(f"y_copied{l}"), i * 4 + (2 * s + 4))
                        act.dma_start(Yd[bass.ds(i * (2 * CAP) + s * CAP, CAP), :], X["ysb"][:, s, :])\
                           .then_inc(sem(f"y_stored{l}_{s}"), 16)
                for s in range(2):
                    act.wait_ge(sem(f"y_stored{l}_{s}"), pairs * 16 + 16)
                    act.sem_inc(sem(f"y_all{l}"), 1)
                end_stage(act, "act")
                norm(f"moe{l}", T, lng[:, 2 * l + 1, :], lnb[:, 2 * l + 1, :])

            project("proj0", PROJ[0], (kraw, kT[:, 4:6, :], 512))
            attention("att0")
            subln()
            gated("mix0", 0, 512)
            norm("mix0", 512, lng[:, 0, :], lnb[:, 0, :])
            moe(0)
            project("proj1", PROJ[1], (kraw, kT[:, 4:6, :], 512), rpb=True)
            attention("att1")
            gated("mix1", 1, TS)
            norm("mix1", TS, lng[:, 2, :], lnb[:, 2, :])
            moe(1)
            for l in range(DEPTH):
                project(f"proj2_{l}", PROJ2, (kraw2, kd2, TS))
                attention(f"att2_{l}")
                tag = f"branch_{l}"
                for b in range(3):
                    for m in range(KC):
                        act.wait_ge(*at(tag, "mm", 2 * b * KC + m + 1))
                        if b:
                            act.wait_ge(*at(tag, "merged", (b - 1) * KC + m + 1))
                        act.activation(G2[:, m, :], PS[:, m, 0:TS], ACT.Sigmoid).then_inc(sig(tag, "gates"), 1)
                end_stage(act, "act")
                norm(f"mix2_{l}", TS, lng2[:, 2 * l, :], lnb2[:, 2 * l, :])
                tag = f"ffn_{l}"
                for k in range(FC):
                    j, m = divmod(k, 4)
                    act.wait_ge(*at(tag, "mm", 8 * j + m + 1))
                    if k >= 4:
                        act.wait_ge(*at(tag, "hid", k - 3))
                    act.activation(sg2[:, m, :], PS[:, m, 0:TS], ACT.Silu).then_inc(sig(tag, "silu"), 1)
                end_stage(act, "act")
                norm(f"down_{l}", TS, lng2[:, 2 * l + 1, :], lnb2[:, 2 * l + 1, :])
            act.dma_start(out, h[:, 0]).then_inc(sem("out_stored"), 16)
            act.wait_ge(sem("out_stored"), 16)

        @block.vector
        def _(dve):
            link = Chain(dve, "dve_link")
            dve.wait_ge(sem("params"), 16 * 16)
            lv = carve(0, 4, HD)
            link(dve.tensor_tensor(carve(256, 2, HD), lv[:, 0:4:2, :], lv[:, 1:4:2, :], ALU.mult))
            dve.tensor_reduce(neglam[:, 1:3], carve(256, 2, HD), AX.X, ALU.add).then_inc(sem("lam_dot"), 1)
            dve.wait_ge(sem("lam_exp"), 1)
            link(dve.tensor_tensor(neglam[:, 3:4], neglam[:, 2:3], neglam[:, 1:2], ALU.subtract))
            link(dve.tensor_scalar(neglam[:, 0:1], neglam[:, 3:4], -LAM_INIT, None, ALU.add))
            dve.wait_ge(sem("mods_mm"), 24)
            for l in range(DEPTH):
                link(dve.tensor_tensor(mods[:, l, :, :], PS[:, l, 0:96].rearrange("p (j s) -> p j s", s=2),
                                       modb[:, l, :].unsqueeze(2).to_broadcast([P, 48, 2]), ALU.add))
                for k in (1, 4):
                    link(dve.tensor_scalar(mods[:, l, k * KC:k * KC + KC, :], mods[:, l, k * KC:k * KC + KC, :],
                                           1.0, None, ALU.add))

            def modulate(l, shift, T, tag=None):
                for c in range(KC):
                    if tag:
                        dve.wait_ge(*at(tag, "normed", c + 1))
                    for s in range(T // TS):
                        dve.tensor_scalar(a[:, s, c, :], h[:, s, c, :], mods[:, l, (shift + 1) * KC + c, s:s + 1],
                                          mods[:, l, shift * KC + c, s:s + 1], ALU.mult, ALU.add)

            modulate(0, 0, 512)
            end_stage(dve, "dve")

            def project(tag, L):
                n_rms = n_rope = 0
                for g, e in enumerate(L):
                    if e["rms"] is not None:
                        dve.wait_ge(*at(tag, "root", n_rms + 1))
                        link(dve.reciprocal(rs_b[:, n_rms % 2, :], rs_b[:, n_rms % 2, :]))
                        dve.scalar_tensor_tensor(out=e["dst"], in0=e["dst"], scalar=qkg[:, e["rms"]:e["rms"] + 1],
                                                 in1=rs_b[:, n_rms % 2, :], op0=ALU.mult, op1=ALU.mult)\
                           .then_inc(sig(tag, "normed"), 1)
                        n_rms += 1
                    if e["rope"]:
                        d = e["dst"][:, 0:TS]
                        b = rp_b[:, n_rope % 2, :]
                        dve.wait_ge(*at(tag, "rotated", n_rope + 1))
                        dve.tensor_tensor(b, PS[:, 6 + n_rope % 2, 0:TS], C("sin"), ALU.mult)
                        link(dve.tensor_tensor(d, d, C("cos"), ALU.mult))
                        dve.tensor_tensor(d, d, b, ALU.add).then_inc(sig(tag, "roped"), 1)
                        n_rope += 1

            def attention(stage):
                U = UNITS[stage]
                B = att_bufs(ATT)
                S8 = lambda base, j: small[:, base + j % 8:base + j % 8 + 1]
                for i in range(len(U) + 1):
                    if i < len(U):
                        u = U[i]
                        n = u["n"]
                        for j in range(u["j0"], u["j1"]):
                            dve.wait_ge(*at(stage, "scores", j + 1))
                            src = PS[:, j % 4, 0:n]
                            if u["mask"]:
                                if j >= 2:
                                    dve.wait_ge(*at(stage, "exp", j - 1))
                                mk, mn, mul = u["mask"]
                                if mn < n:
                                    dve.tensor_copy(B["Sm"][:, j % 2, mn:n], PS[:, j % 4, mn:n])
                                link(dve.scalar_tensor_tensor(out=B["Sm"][:, j % 2, 0:mn], in0=mk, scalar=mul,
                                                              in1=PS[:, j % 4, 0:mn], op0=ALU.mult, op1=ALU.add))
                                src = B["Sm"][:, j % 2, 0:n]
                            link(dve.tensor_reduce(S8(0, j), src, AX.X, ALU.max))
                            if u["sink"] is not None:
                                link(dve.tensor_scalar(S8(0, j), S8(0, j), SCALE, u["sink"], ALU.mult, ALU.max))
                                dve.tensor_scalar(S8(8, j), S8(0, j), -1.0, None, ALU.mult).then_inc(sig(stage, "max"), 1)
                            else:
                                dve.tensor_scalar(S8(8, j), S8(0, j), -SCALE, None, ALU.mult).then_inc(sig(stage, "max"), 1)
                    if i >= 1:
                        u = U[i - 1]
                        n = u["n"]
                        for k, j in enumerate(range(u["j0"], u["j1"])):
                            dve.wait_ge(*at(stage, "exp", j + 1))
                            if u["sink"] is not None:
                                link(dve.tensor_tensor(S8(16, j), S8(16, j), S8(24, j), ALU.add))
                            link(dve.reciprocal(S8(32, j), S8(16, j)))
                            p = B["Pm"][:, j % 4, 0:n]
                            if not u["diff"]:
                                dve.tensor_scalar(p, p, S8(32, j), None, ALU.mult).then_inc(sig(stage, "probs"), 1)
                            elif k == 0:
                                link(dve.tensor_scalar(p, p, S8(32, j), None, ALU.mult))
                            else:
                                link(dve.tensor_scalar(S8(40, j), S8(32, j), neglam[:, 0:1], None, ALU.mult))
                                p0 = B["Pm"][:, (j - 1) % 4, 0:n]
                                dve.scalar_tensor_tensor(out=p0, in0=p, scalar=S8(40, j), in1=p0, op0=ALU.mult, op1=ALU.add)\
                                   .then_inc(sig(stage, "probs"), 1)
                end_stage(dve, "dve")

            def subln():
                for m in range(4):
                    dve.wait_ge(sem("subln_root"), m + 1)
                    r = carve(2048 + m * 512, 512)
                    link(dve.reciprocal(r, r))
                    link(dve.scalar_tensor_tensor(out=oT[:, m, :], in0=oT[:, m, :], scalar=subg[:, 0:1], in1=r,
                                                  op0=ALU.mult, op1=ALU.mult))
                    dve.tensor_scalar(oT[:, m, :], oT[:, m, :], 1.0 - LAM_INIT, None, ALU.mult)
                end_stage(dve, "dve")

            def residual(tag, T, gated):
                for g in range(KC):
                    if gated:
                        dve.wait_ge(*at(tag, "gated", g + 1))
                        o = carve(13824 + (g % 2) * 512, T)
                    else:
                        dve.wait_ge(*at(tag, "mm", g + 1))
                        o = PS[:, g, 0:T]
                    if T == 512:
                        o = o.rearrange("p (s t) -> p s t", s=2)
                    dve.scalar_tensor_tensor(out=hv(T, g), in0=hv(T, g), scalar=ALPHA, in1=o, op0=ALU.mult, op1=ALU.add)\
                       .then_inc(sig(tag, "z"), 1)

            def norm(tag, T):
                dve.wait_ge(*at(tag, "mean", 1))
                o = PS[:, 0, 0:T]
                if T == 512:
                    o = o.rearrange("p (s t) -> p s t", s=2)
                for c in range(KC):
                    dve.tensor_tensor(hv(T, c), hv(T, c), o, ALU.subtract).then_inc(sig(tag, "centred"), 1)
                dve.wait_ge(*at(tag, "std", 1))
                link(dve.reciprocal(carve(14848, T), carve(14848, T)))
                r = carve(14848, T)
                if T == 512:
                    r = r.rearrange("p (s t) -> p s t", s=2)
                for c in range(KC):
                    dve.tensor_tensor(hv(T, c), hv(T, c), r, ALU.mult).then_inc(sig(tag, "scaled"), 1)

            def moe(l):
                T = 512 if l == 0 else TS
                nt = T // P
                L, f, A3 = R["L"][:, 0:nt], R["f"], R["A"]
                dve.wait_ge(sem("router_weights"), 48 * (l + 1))
                dve.wait_ge(sem("logits"), l + 1)
                link(dve.tensor_tensor(L, PS[:, 0, 0:36 * nt].rearrange("p (t e) -> p t e", e=36),
                                       bgr[:, :].unsqueeze(1).to_broadcast([P, nt, 36]), ALU.add))
                link(dve.memset(R["g8"][:, 0:nt, :], NEG))
                link(dve.tensor_copy(R["g8"][:, 0:nt, 0:4], L[:, :, 0:4]))
                for t in range(nt):
                    link(dve.max(R["gmx"][:, t, :], R["g8"][:, t, :]))
                    link(dve.max_index(gidx[:, t, :], R["gmx"][:, t, :], R["g8"][:, t, :]))
                dve.tensor_tensor(R["ge"][:, 0:nt, :], L[:, :, 0:4], R["gmx"][:, 0:nt, 0:1].to_broadcast([P, nt, 4]),
                                  ALU.subtract).then_inc(sem("group_max"), 1)
                link(dve.tensor_copy(f[:, 0, 0:nt], gidx[:, 0:nt, 0]))
                link(dve.tensor_tensor(R["ohg"][:, 0:nt, :], C("iota")[:, 0:4].unsqueeze(1).to_broadcast([P, nt, 4]),
                                       f[:, 0, 0:nt].unsqueeze(2).to_broadcast([P, nt, 4]), ALU.is_equal))
                em = R["em"][:, 0:nt, :].rearrange("p t (g e) -> p t g e", g=4)
                for t in range(nt):
                    link(dve.tensor_tensor(em[:, t], L[:, t, 4:36].rearrange("p (g e) -> p g e", g=4),
                                           R["ohg"][:, t, :].unsqueeze(2).to_broadcast([P, 4, 8]), ALU.mult))
                link(dve.tensor_scalar(R["ohg"][:, 0:nt, :], R["ohg"][:, 0:nt, :], -NEG, NEG, ALU.mult, ALU.add))
                for t in range(nt):
                    link(dve.tensor_tensor(em[:, t], em[:, t], R["ohg"][:, t, :].unsqueeze(2).to_broadcast([P, 4, 8]), ALU.add))
                    link(dve.max(R["emx"][:, t, :], R["em"][:, t, :]))
                    link(dve.max_index(eidx[:, t, :], R["emx"][:, t, :], R["em"][:, t, :]))
                dve.tensor_tensor(f[:, 2, 0:nt], R["emx"][:, 0:nt, 1], R["emx"][:, 0:nt, 0], ALU.subtract)\
                   .then_inc(sem("pair_diff"), 1)
                for k in range(2):
                    link(dve.tensor_copy(f[:, 4 + k, 0:nt], eidx[:, 0:nt, k]))
                    link(dve.tensor_tensor(A3[k][:, 0:nt, :], C("iota").unsqueeze(1).to_broadcast([P, nt, NE]),
                                           f[:, 4 + k, 0:nt].unsqueeze(2).to_broadcast([P, nt, NE]), ALU.is_equal))
                dve.tensor_tensor(A3[2][:, 0:nt, :], A3[0][:, 0:nt, :], A3[1][:, 0:nt, :], ALU.add)\
                   .then_inc(sem("chosen"), 1)
                dve.wait_ge(sem("group_exp"), l + 1)
                link(dve.tensor_reduce(f[:, 3, 0:nt], R["ge"][:, 0:nt, :], AX.X, ALU.add))
                link(dve.reciprocal(f[:, 3, 0:nt], f[:, 3, 0:nt]))
                dve.wait_ge(sem("pair_exp"), l + 1)
                link(dve.tensor_scalar(f[:, 6, 0:nt], f[:, 2, 0:nt], 1.0, None, ALU.add))
                link(dve.reciprocal(f[:, 6, 0:nt], f[:, 6, 0:nt]))
                link(dve.tensor_tensor(w12[:, 0, 0:nt], f[:, 6, 0:nt], f[:, 3, 0:nt], ALU.mult))
                link(dve.tensor_tensor(w12[:, 1, 0:nt], f[:, 2, 0:nt], w12[:, 0, 0:nt], ALU.mult))
                dve.wait_ge(sem("ranks"), l + 1)
                cnt = PS[:, 2, 0:NE]
                link(dve.tensor_scalar(R["ovf"], cnt, float(CAP), None, ALU.is_gt))
                for k in (2, 3):
                    link(dve.tensor_scalar(R["ob"], cnt, float(k * CAP), None, ALU.is_gt))
                    link(dve.tensor_tensor(R["ovf"], R["ovf"], R["ob"], ALU.add))
                link(dve.memset(R["cum"][:, 0:16], 0.0))
                link(dve.memset(R["cum2"][:, 0:16], 0.0))
                link(dve.tensor_copy(R["cum"][:, 16:48], R["ovf"]))
                x, y = R["cum"], R["cum2"]
                for sh in (1, 2, 4, 8, 16):
                    link(dve.tensor_tensor(y[:, 16:48], x[:, 16:48], x[:, 16 - sh:48 - sh], ALU.add))
                    x, y = y, x
                end = x[:, 16:48]
                link(dve.tensor_tensor(R["ob"], end, R["ovf"], ALU.subtract))
                for k in range(2):
                    r, o, q, t_, u_ = (f[:, i, 0:nt] for i in (7, 8, 9, 10, 11))
                    link(dve.tensor_tensor(R["tmp"][:, 0:nt, :], A3[k][:, 0:nt, :],
                                           PS[:, 1, 0:NE * nt].rearrange("p (t e) -> p t e", e=NE), ALU.mult))
                    link(dve.tensor_reduce(r, R["tmp"][:, 0:nt, :], AX.X, ALU.add))
                    link(dve.tensor_tensor(R["tmp"][:, 0:nt, :], A3[k][:, 0:nt, :],
                                           R["ob"].unsqueeze(1).to_broadcast([P, nt, NE]), ALU.mult))
                    link(dve.tensor_reduce(o, R["tmp"][:, 0:nt, :], AX.X, ALU.add))
                    link(dve.tensor_scalar(t_, r, float(CAP), None, ALU.is_ge))
                    link(dve.tensor_copy(q, t_))
                    for z in (2, 3):
                        link(dve.tensor_scalar(u_, r, float(z * CAP), None, ALU.is_ge))
                        link(dve.tensor_tensor(q, q, u_, ALU.add))
                    link(dve.tensor_tensor(o, o, q, ALU.add))
                    link(dve.scalar_tensor_tensor(out=o, in0=o, scalar=float(NE - 1), in1=f[:, 4 + k, 0:nt],
                                                  op0=ALU.add, op1=ALU.subtract))
                    link(dve.tensor_tensor(o, o, t_, ALU.mult))
                    link(dve.tensor_tensor(o, o, f[:, 4 + k, 0:nt], ALU.add))
                    link(dve.tensor_tensor(o, o, q, ALU.subtract))
                    link(dve.scalar_tensor_tensor(out=r, in0=o, scalar=float(CAP), in1=r, op0=ALU.mult, op1=ALU.add))
                    dve.tensor_copy(dest_i[:, k, 0:nt], r).then_inc(sem(f"dest{l}"), 1)
                J = NTAB - NE
                link(dve.tensor_tensor(R["jt"], end.unsqueeze(1).to_broadcast([P, J, NE]),
                                       C("jota").unsqueeze(2).to_broadcast([P, J, NE]), ALU.is_le))
                link(dve.tensor_reduce(R["tabf"][:, NE:NTAB], R["jt"], AX.X, ALU.add))
                link(dve.tensor_scalar(R["tabf"][:, NE:NTAB], R["tabf"][:, NE:NTAB], float(NE - 1), None, ALU.min))
                link(dve.tensor_copy(R["tabf"][:, 0:NE], C("iota")))
                link(dve.tensor_copy(tab_i[0:1, :], R["tabf"][0:1, :]))
                tot = end[:, NE - 1:NE]
                link(dve.tensor_scalar(f[:, 12, 0:1], tot, 0.5, float(NE // 2), ALU.is_gt, ALU.add))
                for z in (2.5, 4.5, 6.5):
                    link(dve.tensor_scalar(f[:, 13, 0:1], tot, z, None, ALU.is_gt))
                    link(dve.tensor_tensor(f[:, 12, 0:1], f[:, 12, 0:1], f[:, 13, 0:1], ALU.add))
                link(dve.tensor_scalar(f[:, 12, 1:2], f[:, 12, 0:1], 2.0, -1.0, ALU.mult, ALU.add))
                dve.tensor_copy(np_i[0:1, :], f[0:1, 12, 0:2]).then_inc(sem(f"routed{l}"), 1)
                dve.wait_ge(sem("slots_turned"), l + 1)
                dve.tensor_copy(tok_i[:, :], PS[:, 3, 0:NTAB]).then_inc(sem(f"routed{l}"), 1)
                dve.wait_ge(sem(f"routed{l}"), 2)
                pairs = dve.value_load(np_i[0:1, 0:1], min_val=NE // 2, max_val=20)
                with dve.Fori(0, pairs) as i:
                    for s in range(2):
                        dve.wait_ge(sem(f"silu{l}"), i * 2 + (s + 1))
                        dve.wait_ge(sem(f"w3_done{l}"), i * 2 + (s + 1))
                        dve.tensor_tensor(X["hid"], X["sil"], PS[:, 3, :], ALU.mult).then_inc(sem(f"hidden{l}"), 1)
                        dve.wait_ge(sem(f"hidden_turned{l}"), i * 2 + (s + 1))
                        dve.tensor_copy(X["hidT"], PS[:, 4, :].rearrange("p (c t) -> p c t", c=4))\
                           .then_inc(sem(f"hidden_ready{l}"), 1)
                        dve.wait_ge(sem(f"w2_done{l}"), i * 2 + (s + 1))
                        dve.wait_ge(sem(f"y_stored{l}_{s}"), i * 16 + 16)
                        dve.tensor_copy(X["ysb"][:, s, 512:1024], PS[:, 7, :]).then_inc(sem(f"y_copied{l}"), 1)
                end_stage(dve, "dve")
                for tt in range(nt):
                    b = tt % 2
                    dve.wait_ge(sem(f"y_gathered{l}_{b}"), 32 * (tt // 2 + 1))
                    link(dve.tensor_scalar(X["y1"][:, b, :], X["y1"][:, b, :], w12[:, 0, tt:tt + 1], None, ALU.mult))
                    dve.scalar_tensor_tensor(out=X["y1"][:, b, :], in0=X["y2"][:, b, :], scalar=w12[:, 1, tt:tt + 1],
                                             in1=X["y1"][:, b, :], op0=ALU.mult, op1=ALU.add).then_inc(sem(f"mixed{l}"), 1)
                    for hf in range(2):
                        k = 2 * tt + hf
                        dve.wait_ge(sem(f"moe{l}_back"), k + 1)
                        ps = PS[:, 2 + k % 4, :].rearrange("p (c t) -> p c t", c=4)
                        tz = X["tz"][:, k % 2, :].rearrange("p (c t) -> p c t", c=4)
                        s = tt // 2
                        hh = h[:, s, 4 * hf:4 * hf + 4, (tt % 2) * P:(tt % 2) * P + P]
                        gate = mods[:, l, 5 * KC + 4 * hf:5 * KC + 4 * hf + 4, s:s + 1]
                        link(dve.tensor_tensor(tz, ps, gate.to_broadcast([P, 4, P]), ALU.mult))
                        dve.scalar_tensor_tensor(out=hh, in0=hh, scalar=ALPHA, in1=tz, op0=ALU.mult, op1=ALU.add)\
                           .then_inc(sig(f"moe{l}", "z"), 1)
                norm(f"moe{l}", T)
                if l == 0:
                    modulate(1, 0, 512, "moe0")
                end_stage(dve, "dve")

            project("proj0", PROJ[0])
            end_stage(dve, "dve")
            attention("att0")
            subln()
            residual("mix0", 512, True)
            norm("mix0", 512)
            modulate(0, 3, 512, "mix0")
            end_stage(dve, "dve")
            moe(0)
            project("proj1", PROJ[1])
            dve.wait_ge(sem("rpb_loaded"), 16 * 16)
            for hn in range(8):
                dve.scalar_tensor_tensor(out=rpbT[:, :, hn, :], in0=rpbT[:, :, hn, :], scalar=1.0 / SCALE,
                                         in1=CR("nbhd", 2), op0=ALU.mult, op1=ALU.add)
            end_stage(dve, "dve")
            attention("att1")
            residual("mix1", TS, True)
            norm("mix1", TS)
            modulate(1, 3, TS, "mix1")
            end_stage(dve, "dve")
            moe(1)
            for l in range(DEPTH):
                dve.wait_ge(*at(f"proj2_{l}", "evacuated", 19))
                link(dve.tensor_tensor(bc2, bc2, bh2, ALU.mult))
                for m in range(4):
                    u, o = bc2[:, m, :], cv2[:, m, :]
                    link(dve.tensor_scalar(o, u, convw[:, l, 2, m:m + 1], None, ALU.mult))
                    link(dve.scalar_tensor_tensor(out=o[:, 1:TS], in0=u[:, 0:TS - 1], scalar=convw[:, l, 1, m:m + 1],
                                                  in1=o[:, 1:TS], op0=ALU.mult, op1=ALU.add))
                    link(dve.scalar_tensor_tensor(out=o[:, 2:TS], in0=u[:, 0:TS - 2], scalar=convw[:, l, 0, m:m + 1],
                                                  in1=o[:, 2:TS], op0=ALU.mult, op1=ALU.add))
                dve.tensor_tensor(cv2, cv2, bb2, ALU.mult)
                end_stage(dve, "dve")
                attention(f"att2_{l}")
                tag = f"branch_{l}"
                for b in range(3):
                    for m in range(KC):
                        dve.wait_ge(*at(tag, "gates", b * KC + m + 1))
                        dve.wait_ge(*at(tag, "mm", (2 * b + 1) * KC + m + 1))
                        if b == 0:
                            dve.tensor_tensor(M2[:, m, :], G2[:, m, :], PS[:, m, 0:TS], ALU.mult)\
                               .then_inc(sig(tag, "merged"), 1)
                        else:
                            link(dve.tensor_tensor(mt2[:, m % 2, :], G2[:, m, :], PS[:, m, 0:TS], ALU.mult))
                            dve.tensor_tensor(M2[:, m, :], M2[:, m, :], mt2[:, m % 2, :], ALU.add)\
                               .then_inc(sig(tag, "merged"), 1)
                end_stage(dve, "dve")
                residual(f"mix2_{l}", TS, False)
                norm(f"mix2_{l}", TS)
                end_stage(dve, "dve")
                tag = f"ffn_{l}"
                for k in range(FC):
                    j, m = divmod(k, 4)
                    nm = min(4, FC - 4 * j)
                    dve.wait_ge(*at(tag, "silu", k + 1))
                    dve.wait_ge(*at(tag, "mm", 8 * j + nm + m + 1))
                    dve.tensor_tensor(hid2[:, k, :], sg2[:, m, :], PS[:, 4 + m, 0:TS], ALU.mult).then_inc(sig(tag, "hid"), 1)
                end_stage(dve, "dve")
                dve.wait_ge(sem(f"down_{l}"), 6)
                for g in range(KC):
                    dve.scalar_tensor_tensor(out=h[:, 0, g, :], in0=h[:, 0, g, :], scalar=ALPHA, in1=PS[:, g, 0:TS],
                                             op0=ALU.mult, op1=ALU.add).then_inc(sig(f"down_{l}", "z"), 1)
                norm(f"down_{l}", TS)
                end_stage(dve, "dve")

        @block.gpsimd
        def _(pool):
            link = Chain(pool, "pool_link")

            def idle(n):
                for _ in range(n):
                    end_stage(pool, "pool")

            def moe(l):
                T = 512 if l == 0 else TS
                nt = T // P
                for s in range(2):
                    pool.sem_inc(sem(f"y_stored{l}_{s}"), 16)
                pool.sem_inc(sem(f"y_copied{l}"), 2)
                pool.sem_inc(sem(f"x_turned{l}"), 1)
                link(pool.memset(R["zero"], 0.0))
                pool.dma_start(tokd.rearrange("(b s) o -> b (s o)", s=CAP), R["zero"]).then_inc(sem(f"slots_zero{l}"), 16)
                pool.wait_ge(sem(f"slots_zero{l}"), 16)
                pool.wait_ge(sem(f"dest{l}"), 2)
                for k in range(2):
                    for tt in range(nt):
                        pool.indirect_dma_start(out=tokd, out_offset=bass.IndirectOffsetOnAxis(ap=dest_i[:, k, tt:tt + 1], axis=0),
                                                in_=C("token")[:, tt:tt + 1], in_offset=None)\
                            .then_inc(sem(f"slots_set{l}"), 16)
                pool.wait_ge(sem(f"slots_set{l}"), 16 * 2 * nt)
                pool.dma_start(R["tokrow"], tokd.rearrange("(b s) o -> b (s o)", s=CAP)).then_inc(sem(f"slots_back{l}"), 16)
                for b in range(2):
                    pool.wait_ge(sem(f"rows{l}_stored_{b}"), 16 * (nt // 2))
                pool.wait_ge(sem(f"routed{l}"), 2)
                pairs = pool.value_load(np_i[0:1, 0:1], min_val=NE // 2, max_val=20)

                def gather(b1):
                    pool.indirect_dma_start(out=X["xg"][:, b1, :], out_offset=None, in_=Fd,
                                            in_offset=bass.IndirectOffsetOnAxis(ap=gat[:, b1:b1 + 1], axis=0))\
                        .then_inc(sem(f"gathered{l}_{b1}"), 16)

                pool.tensor_copy(gat[:, 0:1], tok_i[:, 0:1]).then_inc(sem(f"index{l}"), 1)
                pool.wait_ge(sem(f"index{l}"), 1)
                gather(0)
                with pool.Fori(0, pairs) as i:
                    for s in range(2):
                        pool.wait_ge(sem(f"x_turned{l}"), i * 2 + (s + 1))
                        pool.sem_inc(sem(f"pool_step{l}"), 1)
                        pool.tensor_copy(gat[:, 1 - s:2 - s], tok_i[:, bass.ds(i * 2 + (s + 1), 1)]).then_inc(sem(f"index{l}"), 1)
                        pool.wait_ge(sem(f"index{l}"), i * 2 + (s + 2))
                        pool.sem_inc(sem(f"pool_step{l}"), 1)
                        gather(1 - s)
                end_stage(pool, "pool")
                pool.wait_ge(sem(f"y_all{l}"), 2)
                for tt in range(nt):
                    b = tt % 2
                    if tt >= 2:
                        pool.wait_ge(sem(f"moe{l}_back"), 2 * (tt - 1))
                    for k, y in enumerate((X["y1"], X["y2"])):
                        pool.indirect_dma_start(out=y[:, b, :], out_offset=None, in_=Yd,
                                                in_offset=bass.IndirectOffsetOnAxis(ap=dest_i[:, k, tt:tt + 1], axis=0))\
                            .then_inc(sem(f"y_gathered{l}_{b}"), 16)
                end_stage(pool, "pool")

            pool.memset(carve(8192, D), 0.0).then_inc(sem("zero_rows"), 1)
            pool.wait_ge(sem("zero_rows"), 1)
            for b in range(NE, NBLK):
                pool.dma_start(Yd[b * CAP:b * CAP + CAP, :], carve(8192, D)).then_inc(sem("spill_zeroed"), 16)
            pool.wait_ge(sem("spill_zeroed"), 16 * (NBLK - NE))
            idle(1)
            idle(4)
            moe(0)
            idle(3)
            moe(1)
            idle(2 * 6)

        @block.sync
        def _(sp):
            def load(seq):
                g, slot, n, k = slot_of(seq)
                name, view, src = tiles[seq]
                sp.dma_start(view(ring[:, slot, :]), src).then_inc(loaded(g, slot), 16)

            def expert(l, s, e, r0):
                for k, w in enumerate(("moe_w1", "moe_w3", "moe_w2")):
                    c = 4 if k == 2 else KC
                    if isinstance(e, int):
                        src = A[w][l, e].rearrange("(c p) n -> p c n", c=c)
                    else:
                        src = A[w][l, bass.ds(e, 1)].rearrange("a (c p) n -> p (a c) n", c=c)
                    yield k, ring[:, (r0 + 3 * s + k) % RING, :].rearrange("p (c n) -> p c n", c=c), src

            pairs = None
            for g in range(3):
                for seq in range(SEG[g], SEG[g + 1]):
                    k = seq - SEG[g]
                    if g == 0 and k >= RING:
                        sp.wait_ge(*used[seq - RING])
                    elif g > 0 and k < RING:
                        l = g - 1
                        s = ("w1_done", "w3_done", "w2_done")[k % 3]
                        sp.wait_ge(sem(f"{s}{l}"), last if k < 3 else last + 1)
                    elif g > 0:
                        sp.wait_ge(*used[seq - RING])
                    load(seq)
                if g < 2:
                    l, r0 = g, SEG[g + 1] % RING
                    for s in range(2):
                        for k, dst, src in expert(l, s, s, r0):
                            sp.wait_ge(*used[SEG[g + 1] + 3 * s + k - RING])
                            sp.dma_start(dst, src).then_inc(moe_loaded(l, (r0 + 3 * s + k) % RING), 16)
                    sp.wait_ge(sem(f"routed{l}"), 2)
                    pairs = sp.value_load(np_i[0:1, 0:1], min_val=NE // 2, max_val=20)
                    last = sp.value_load(np_i[0:1, 1:2], min_val=NE - 1, max_val=39)
                    with sp.Fori(0, pairs - 1) as i:
                        for s in range(2):
                            e = sp.value_load(tab_i[0:1, bass.ds(i * 2 + (s + 2), 1)], min_val=0, max_val=NE - 1)
                            for k, dst, src in expert(l, s, e, r0):
                                done = ("w1_done", "w3_done", "w2_done")[k]
                                sp.wait_ge(sem(f"{done}{l}"), i * 2 + (s + 1))
                                sp.dma_start(dst, src).then_inc(moe_loaded(l, (r0 + 3 * s + k) % RING), 16)


def kernel(**inputs):
    import concourse.bacc as _bacc
    from concourse.bass_utils import run_bass_kernel_spmd as _run

    def get(n):
        return np.asarray(inputs[n])

    def chunks(v):
        v = v.reshape(v.shape[:-1] + (-1, P))
        return np.moveaxis(v, -1, 0)

    arrays = {
        "consts": CONST_ARRAY,
        "cT": np.stack([chunks(get("c")[0]), chunks(get("c_ctx"))], -1).reshape(P, 16),
        "xT": np.swapaxes(chunks(get("x")[0]), 1, 2),
        "ctxT": np.swapaxes(chunks(get("ctx")[0]), 1, 2),
        "mod_w": get("mod_w"), "mod_bT": chunks(get("mod_b")),
        "ln_gT": chunks(get("ln_g").reshape(4, D)), "ln_bT": chunks(get("ln_b").reshape(4, D)),
        "ln_g2T": chunks(np.stack([get("ln1_g_2"), get("ln2_g_2")], 1).reshape(4, D)),
        "ln_b2T": chunks(np.stack([get("ln1_b_2"), get("ln2_b_2")], 1).reshape(4, D)),
        "sublnT": get("diff_subln_g").reshape(P, 1), "qkgT": get("gqa_qk_g")[0].T,
        "win_sink": get("win_sink").reshape(1, 8), "attn_sinks": get("attn_sinks_2").reshape(1, 16),
        "convT": chunks(get("conv_w_2")), "diff_lambda": get("diff_lambda").reshape(1, 256),
        "ab_w_in": get("ab_w_in"), "ab_w_out": get("ab_w_out"), "cd_w_in": get("cd_w_in"), "cd_w_out": get("cd_w_out"),
        "na_rpb": get("na_rpb"),
        "wgT": np.transpose(get("moe_w_group").reshape(DEPTH, KC, P, 4), (2, 0, 1, 3)),
        "wrT": np.transpose(get("moe_w_router").reshape(DEPTH, KC, P, NE), (2, 0, 1, 3)),
        "bgr": np.concatenate([get("moe_b_group"), get("moe_b_router")], 1),
        "moe_w1": get("moe_w1"), "moe_w3": get("moe_w3"), "moe_w2": get("moe_w2"),
        "w_in_2": get("w_in_2"), "w_branch_a_2": get("w_branch_a_2"), "w_branch_b_2": get("w_branch_b_2"),
        "w_branch_c_2": get("w_branch_c_2"), "w_out_2": get("w_out_2"), "w_ffn_gate_2": get("w_ffn_gate_2"),
        "w_ffn_up_2": get("w_ffn_up_2"), "w_ffn_down_2": get("w_ffn_down_2"),
    }
    nc = _bacc.Bacc("TRN2", target_bir_lowering=False, num_devices=1)
    maps, aps = {}, {}
    for name, v in arrays.items():
        v = np.ascontiguousarray(v)
        maps[f"in_{name}"] = v
        aps[name] = nc.dram_tensor(f"in_{name}", v.shape, mybir.dt.from_np(v.dtype), kind="ExternalInput").ap()
    out = nc.dram_tensor("out_dram", (P, KC, TS), F32, kind="ExternalOutput").ap()
    program(nc, aps, out)
    r = _run(nc, [maps], core_ids=[0])
    return np.ascontiguousarray(np.transpose(r.results[0]["out_dram"], (2, 1, 0)).reshape(1, TS, D))
```

```python
from contextlib import ExitStack

import numpy as np

import concourse.bass as bass
from concourse import mybir

ALU = mybir.AluOpType
ACT = mybir.ActivationFunctionType
AX = mybir.AxisListType
F32 = mybir.dt.float32
I32 = mybir.dt.int32
U32 = mybir.dt.uint32

P = 128
D = 1024
KC = D // P
TS = 256
HD = 64
DEPTH = 2
NE = 32
CAP = 64
FH = 512
RING = 6
NBLK = 48
FFN = 2816
FC = FFN // P
ALPHA = (2.0 * DEPTH) ** 0.25
SCALE = HD ** -0.5
NEG = -1e30
LAM_INIT = 0.2

CONSTS = {}


def build_consts():
    parts, at = [], 0

    def add(name, a):
        nonlocal at
        a = np.asarray(a, np.float32).reshape(P, -1)
        CONSTS[name] = (at, a.shape[1])
        parts.append(a)
        at += a.shape[1]

    p = np.arange(P)
    add("ident", np.eye(P))
    add("ones", np.ones((P, P)))
    add("mean_d", np.full((P, P), 1.0 / D))
    add("mean_p", np.full((P, P), 1.0 / P))
    add("mean_h", (p[:, None] // HD == p[None, :] // HD) / HD)
    add("before", p[:, None] < p[None, :])
    other = np.where(p % HD < HD // 2, p + HD // 2, p - HD // 2)
    add("swap", p[:, None] == other[None, :])
    t = np.arange(TS)
    inv = 10000.0 ** (-np.arange(HD // 4, dtype=np.float32) / np.float32(HD // 4))
    inv = inv.astype(np.float32)
    ang = np.concatenate([(t // 64).astype(np.float32)[:, None] * inv, (t % 64).astype(np.float32)[:, None] * inv], -1)
    cos, sin = np.cos(ang).T, np.sin(ang).T
    add("cos", np.tile(cos, (4, 1)))
    add("sin", np.concatenate([-sin, sin, -sin, sin], 0))
    q = (np.arange(2)[None, :] * P + p[:, None])[:, :, None]
    k = np.arange(TS)[None, None, :]
    add("near", np.where(np.abs(q - k) <= 128, 0.0, NEG))
    col0 = np.clip(q % 64 - 8, 0, 48)
    add("nbhd", np.where((k % 64 >= col0) & (k % 64 < col0 + 16), 0.0, NEG))
    add("swa", np.where((q - k >= 0) & (q - k < 128), k - q, NEG))
    add("causal", np.where(q - k >= 0, k - q, NEG))
    add("iota", np.tile(np.arange(CAP), (P, 1)))
    add("place", np.tile(np.arange(34), (P, 1)))
    add("odd_place", np.tile(np.arange(34) % 2, (P, 1)))
    add("eps_ln", np.full((P, 1), 1e-5))
    add("eps_rms", np.full((P, 1), 1e-6))
    return np.ascontiguousarray(np.concatenate(parts, 1))


CONST_ARRAY = build_consts()


def program(nc, A, out):
    stack = ExitStack()
    with stack:
        def sb(name, shape, dt=F32):
            return stack.enter_context(nc.sbuf_tensor(name, shape, dt))

        sems = {}

        def sem(name):
            if name not in sems:
                sems[name] = stack.enter_context(nc.semaphore(name))
            return sems[name]

        def dram(name, shape, dt=F32):
            return nc.dram_tensor(name, shape, dt, kind="Internal").ap()

        NT = NE + 2
        ring = sb("ring", [P, RING, 4096])
        h = sb("h", [P, 2, KC, TS])
        a = sb("a", [P, 2, KC, TS])
        W = sb("W", [P, 15872])
        cst = sb("cst", [P, CONST_ARRAY.shape[1]])
        cc = sb("cc", [P, KC, 2])
        mods = sb("mods", [P, DEPTH, 6 * KC, 2])
        modb = sb("modb", [P, DEPTH, 6 * KC])
        lng = sb("lng", [P, 4, KC])
        lnb = sb("lnb", [P, 4, KC])
        lng2 = sb("lng2", [P, 4, KC])
        lnb2 = sb("lnb2", [P, 4, KC])
        subg = sb("subg", [P, 1])
        qkg = sb("qkg", [P, 2])
        sinks = sb("sinks", [P, 24])
        convw = sb("convw", [P, DEPTH, 3, 4])
        bgr = sb("bgr", [P, 36])
        neglam = sb("neglam", [P, 4])
        small = sb("small", [P, 64])
        w12 = sb("w12", [P, 2, 4])
        dest_i = sb("dest_i", [P, 2, 4], I32)
        gidx = sb("gidx", [P, 4, 8], U32)
        eidx = sb("eidx", [P, 4, 8], U32)
        sub_i = sb("sub_i", [1, 6, NT], I32)
        np_i = sb("np_i", [1, 1], I32)
        PS = stack.enter_context(nc.psum_tensor("PS", [P, 8, 512], F32))

        Yd = dram("slot_out_dram", [(NBLK + 8) * CAP, D])
        Bd = dram("rpb_dram", [7, 8, 64, 64])

        def C(name):
            o, n = CONSTS[name]
            return cst[:, o:o + n]

        def CR(name, n):
            return C(name).rearrange("p (t k) -> p t k", t=n)

        ident = C("ident")

        def carve(at, *shape):
            n = int(np.prod(shape))
            v = W[:, at:at + n]
            names = "abcd"[:len(shape)]
            if len(shape) > 1:
                v = v.rearrange(f"p ({' '.join(names)}) -> p {' '.join(names)}",
                                **{names[i]: shape[i] for i in range(len(shape) - 1)})
            return v

        tiles = []

        def cols(name, w, n0, n=512):
            tiles.append((name, lambda r, n=n: r[:, 0:KC * n].rearrange("p (c n) -> p c n", c=KC),
                          w[:, n0:n0 + n].rearrange("(c p) n -> p c n", p=P)))

        def rows(name, w, k0, k=512):
            c = k // P
            tiles.append((name, lambda r, c=c: r[:, 0:c * D].rearrange("p (c n) -> p c n", c=c),
                          w[k0:k0 + k, :].rearrange("(c p) n -> p c n", p=P)))

        for j in range(12):
            cols("mod0", A["mod_w"][0], 512 * j)
        seg_start = []
        for l in range(DEPTH):
            w_in, w_o = (A["ab_w_in"][0], A["ab_w_out"][0]) if l == 0 else (A["cd_w_in"][0], A["cd_w_out"][0])
            if l == 0:
                for n0, n in ((0, 512), (512, 512), (1024, 512), (1536, 512), (2048, 256)):
                    cols("in0", w_in, n0, n)
                for j in range(12):
                    cols("mod1", A["mod_w"][1], 512 * j)
            else:
                for n0, n in ((0, 512), (512, 512), (1024, 256), (1280, 512), (1792, 512)):
                    cols("in1", w_in, n0, n)
            cols(f"out{l}", w_o, 0)
            cols(f"out{l}", w_o, 512)
            seg_start.append(len(tiles))
        for l in range(DEPTH):
            w = A["w_in_2"][l]
            for n0, n in ((0, 512), (512, 256), (768, 512), (1280, 512), (1792, 512),
                          (2304, 512), (2816, 512), (3328, 512)):
                cols(f"in2_{l}", w, n0, n)
            for b, br in enumerate("abc"):
                cols(f"gate2_{l}", w, 3840 + D * b)
                cols(f"gate2_{l}", w, 3840 + D * b + 512)
                rows(f"branch2_{l}", A[f"w_branch_{br}_2"][l], 0)
            cols(f"out2_{l}", A["w_out_2"][l], 0)
            cols(f"out2_{l}", A["w_out_2"][l], 512)
            for j in range(6):
                n = min(512, FFN - 512 * j)
                cols(f"ffn_gate_{l}", A["w_ffn_gate_2"][l], 512 * j, n)
                cols(f"ffn_up_{l}", A["w_ffn_up_2"][l], 512 * j, n)
            for j in range(6):
                rows(f"ffn_down_{l}", A["w_ffn_down_2"][l], 512 * j, min(512, FFN - 512 * j))
        SEG = [0, seg_start[0], seg_start[1], len(tiles)]

        def slot_of(seq):
            g = 0 if seq < SEG[1] else 1 if seq < SEG[2] else 2
            k = seq - SEG[g]
            return g, seq % RING, k // RING + 1, k

        def loaded(g, slot):
            return sem(f"tile_loaded_{g}_{slot}")

        def moe_loaded(l, slot):
            return sem(f"expert_tile_loaded_{l}_{slot}")

        used = []

        def engine_loop(eng, start, end):
            return nc.Fori(start, end, engines=[eng.engine], hint_back_edge=True)

        class Chain:

            def __init__(self, eng, name):
                self.eng, self.sem, self.n = eng, sem(name), 0

            def __call__(self, ins):
                self.n += 1
                ins.then_inc(self.sem, 1)
                self.eng.wait_ge(self.sem, self.n)

            def mark(self, ins):
                self.n += 1
                ins.then_inc(self.sem, 1)
                return self.n

            def wait(self, n):
                self.eng.wait_ge(self.sem, n)

        stage_count = {}

        def end_stage(eng, name):
            stage_count[name] = stage_count.get(name, 0) + 1
            eng.drain().then_inc(sem("stage_ended"), 1)
            eng.wait_ge(sem("stage_ended"), 4 * stage_count[name])

        MODS_PS = [PS[:, 0, 0:96], PS[:, 7, 0:96]]

        block = stack.enter_context(nc.Block())

        qT = carve(0, 8, 512)
        q1T = carve(0, 8, TS)
        rpbT = carve(2048, 2, 8, TS)
        kT = carve(6144, 6, 512)
        V = carve(9216, 4, 512)
        VS = carve(11264, 4, P)
        TMP = 11776
        sq_b = carve(TMP, 2, 512)
        rs_b = carve(TMP + 1024, 2, 512)
        rp_b = carve(TMP + 2048, 2, TS)
        kraw = carve(TMP + 2560, 512)
        oT = a[:, 0:2].rearrange("p s c t -> p (s c t)").rearrange("p (c t) -> p c t", c=KC)
        o1T = a[:, 0]

        def proj_list(l):
            L = []

            def feat(tile, m, dst, n, rms=None, rope=False):
                L.append(dict(tile=tile, kind="f", m=m, dst=dst, n=n, rms=rms, rope=rope))

            def toks(tile, c0, n, dst, nt=4):
                for t in range(nt):
                    L.append(dict(tile=tile, kind="t", c0=c0, n=n, tt=t, dst=dst[:, t, 0:n], rms=None, rope=False))

            if l == 0:
                for m in range(4):
                    feat(0, m, qT[:, m, :], 512, None, True)
                for m in range(4):
                    feat(1, m, qT[:, 4 + m, :], 512, 0, True)
                for m in range(4):
                    feat(2, m, kT[:, m, :], 512, None, True)
                toks(3, 0, 512, V)
                feat(4, 0, kraw, 512, 1, True)
                toks(4, P, P, VS)
            elif l == 1:
                for m in range(4):
                    feat(0, m, q1T[:, m, :], TS, None, True)
                for m in range(4):
                    feat(1, m, q1T[:, 4 + m, :], TS)
                feat(2, 0, kraw, 512, None, True)
                toks(2, P, P, VS)
                for m in range(4):
                    feat(3, m, kT[:, m, :], 512)
                toks(4, 0, 512, V)
            return L

        PROJ = [proj_list(0), proj_list(1)]

        qa2 = carve(0, 4, TS)
        qc2 = carve(1024, 4, TS)
        kc2 = carve(2048, 4, TS)
        kd2 = carve(3072, 2, TS)
        kraw2 = carve(3584, TS)
        va2 = carve(3840, 2, P)
        vc2 = carve(4096, 2, 512)
        bh2 = carve(5120, 4, TS)
        bb2 = carve(6144, 4, TS)
        bc2 = carve(7168, 4, TS)
        cv2 = carve(8192, 4, TS)
        ya2 = carve(9216, 4, TS)
        yc2 = carve(10240, 4, TS)
        G2 = carve(0, 8, TS)
        M2 = carve(2048, 8, TS)
        mt2 = carve(11776, 2, TS)
        hid2 = carve(0, FC, TS)
        sg2 = carve(6144, 4, TS)

        def proj2_list():
            L = []
            for t0, dst in ((0, qa2),):
                for m in range(4):
                    L.append(dict(tile=t0, kind="f", m=m, dst=dst[:, m, :], n=TS, rms=None, rope=False))
            L.append(dict(tile=1, kind="f", m=0, dst=kraw2, n=TS, rms=None, rope=False))
            for t in range(2):
                L.append(dict(tile=1, kind="t", c0=P, n=P, tt=t, dst=va2[:, t, :], rms=None, rope=False))
            for t0, dst in ((2, bh2), (3, bb2), (4, bc2), (5, qc2), (6, kc2)):
                for m in range(4):
                    L.append(dict(tile=t0, kind="f", m=m, dst=dst[:, m, :], n=TS, rms=None, rope=False))
            for t in range(2):
                L.append(dict(tile=7, kind="t", c0=0, n=512, tt=t, dst=vc2[:, t, :], rms=None, rope=False))
            return L

        PROJ2 = proj2_list()

        ATT = TMP

        def att_bufs(at):
            return dict(Sm=carve(at, 2, 512), Pm=carve(at + 1024, 4, 512)[:, :, :], PT=carve(at + 3072, 2, 512))

        def halves(k):
            return slice(HD * k, HD * k + HD)

        def units_of(stage):
            U = []
            if stage == "att0":
                for t in range(4):
                    k0 = 0 if t < 2 else TS
                    n = 512 - k0
                    for m in range(4):
                        U.append(dict(comps=[(qT[halves(i), m, t * P:t * P + P], kT[halves(i), m, k0:512]) for i in range(2)],
                                      n=n, mask=None, sink=None, diff=True, pb=0, dv=P,
                                      v=[V[:, k0 // P + kc, m * P:m * P + P] for kc in range(n // P)],
                                      out=oT[:, m, t * P:t * P + P]))
                    for hq in range(8):
                        i = hq % 2
                        kv = hq // 4
                        U.append(dict(comps=[(qT[halves(i), 4 + hq // 2, t * P:t * P + P], kT[halves(i), 4 + kv, k0:512])],
                                      n=n, mask=None, sink=None, diff=False, pb=HD * i, dv=HD,
                                      v=[VS[:, k0 // P + kc, kv * HD:kv * HD + HD] for kc in range(n // P)],
                                      out=oT[halves(i), 4 + hq // 2, t * P:t * P + P]))
            elif stage == "att1":
                for t in range(2):
                    for hq in range(8):
                        i, kv = hq % 2, hq // 4
                        U.append(dict(comps=[(q1T[halves(i), hq // 2, t * P:t * P + P], kT[halves(i), 4 + kv, :])],
                                      n=512, mask=(CR("near", 2)[:, t, :], TS, 1.0), sink=sinks[:, hq:hq + 1],
                                      diff=False, pb=HD * i, dv=HD,
                                      v=[VS[:, kc, kv * HD:kv * HD + HD] for kc in range(4)],
                                      out=o1T[halves(i), hq // 2, t * P:t * P + P]))
                    for hn in range(8):
                        i = hn % 2
                        U.append(dict(comps=[(q1T[halves(i), 4 + hn // 2, t * P:t * P + P], kT[halves(i), hn // 2, :])],
                                      n=512, mask=(rpbT[:, t, hn, :], TS, 1.0), sink=None,
                                      diff=False, pb=HD * i, dv=HD,
                                      v=[V[:, kc, hn * HD:hn * HD + HD] for kc in range(4)],
                                      out=o1T[halves(i), 4 + hn // 2, t * P:t * P + P]))
            else:
                l = int(stage[-1])
                slope = [2.0 ** (-8.0 * (i + 1.0) / 16) for i in range(16)]
                for t in range(2):
                    n = P * (t + 1)
                    for hq in range(8):
                        i, kv = hq % 2, hq // 4
                        U.append(dict(comps=[(qa2[halves(i), hq // 2, t * P:t * P + P], kd2[halves(i), kv, 0:n])],
                                      n=n, mask=(CR("swa", 2)[:, t, 0:n], n, slope[hq] / SCALE),
                                      sink=sinks[:, 8 + 8 * l + hq:9 + 8 * l + hq], diff=False, pb=HD * i, dv=HD,
                                      v=[va2[:, kc, kv * HD:kv * HD + HD] for kc in range(n // P)],
                                      out=ya2[halves(i), hq // 2, t * P:t * P + P]))
                    for hc in range(8):
                        i = hc % 2
                        U.append(dict(comps=[(qc2[halves(i), hc // 2, t * P:t * P + P], kc2[halves(i), hc // 2, 0:n])],
                                      n=n, mask=(CR("causal", 2)[:, t, 0:n], n, slope[8 + hc] / SCALE),
                                      sink=None, diff=False, pb=HD * i, dv=HD,
                                      v=[vc2[:, kc, hc * HD:hc * HD + HD] for kc in range(n // P)],
                                      out=yc2[halves(i), hc // 2, t * P:t * P + P]))
            j = 0
            for u in U:
                u["j0"] = j
                j += len(u["comps"])
                u["j1"] = j
            return U

        UNITS = {s: units_of(s) for s in ("att0", "att1", "att2_0", "att2_1")}
        NO = dict(att0=1, att1=2, att2_0=2, att2_1=2)
        comp_unit = {s: [u for u, x in enumerate(UNITS[s]) for _ in x["comps"]] for s in UNITS}

        def hv(T, c, buf=None):
            b = h if buf is None else buf
            return b[:, :, c, :] if T == 512 else b[:, 0, c, :]

        X = dict(xrow=carve(0, 4, D), xe=carve(4096, KC, CAP), hid=carve(4608, 512), sil=carve(5120, 512),
                 hidT=carve(5632, 4, CAP), ysb=carve(5888, 2, 512), sel=carve(6912, 4, CAP),
                 y1=carve(7680, 2, D), y2=carve(9728, 2, D), tz=carve(11776, 2, 512))
        rb = 12800
        R = {}
        for name, shape in (("L", (4, 36)), ("g8", (4, 8)), ("gmx", (4, 8)), ("ohg", (4, 4)), ("ge", (4, 4)),
                            ("em", (4, 32)), ("emx", (4, 8)), ("A1", (4, 32)), ("A2", (4, 32)), ("AB", (4, 32)),
                            ("tmp", (4, 32)), ("f", (16, 4)), ("ovf", (32,)), ("has", (32,)), ("pos", (32,)), ("cum", (48,)), ("cum2", (48,)),
                            ("ob", (32,)), ("dd", (2, 4)), ("subf", (6, NT)), ("par", (32,)), ("wgr", (KC, 36))):
            R[name] = carve(rb, *shape)
            rb += int(np.prod(shape))
        R["A"] = [R["A1"], R["A2"], R["AB"]]
        assert rb <= 15872, rb
        wgr = R["wgr"]

        def proj_total(L):
            nr, np_ = sum(e["rms"] is not None for e in L), sum(e["rope"] for e in L)
            return dict(mm=len(L), evacuated=len(L), squared=nr, stat=nr, root=nr, normed=nr, rotated=np_, roped=np_)

        def att_total(s):
            u, j = len(UNITS[s]), len(comp_unit[s])
            return dict(scores=j, max=j, exp=j, probs=u, transposed=u, turned=u, pv=u, out=u)

        NORM = dict(mean=1, squared=KC, var=KC, std=1, centred=KC, scaled=KC, normed=KC)
        MIX = dict(NORM, mm=KC, gated=KC, z=KC)
        FAMILIES = {
            "projection": [("proj0", proj_total(PROJ[0])), ("proj1", proj_total(PROJ[1])),
                           ("proj2_0", proj_total(PROJ2)), ("proj2_1", proj_total(PROJ2))],
            "attention": [(s, att_total(s)) for s in ("att0", "att1", "att2_0", "att2_1")],
            "norm": [("mix0", MIX), ("moe0", dict(NORM, mm=0, gated=0, z=8)), ("mix1", MIX),
                     ("moe1", dict(NORM, mm=0, gated=0, z=4)),
                     ("mix2_0", dict(MIX, gated=0)), ("down_0", dict(NORM, mm=0, gated=0, z=KC)),
                     ("mix2_1", dict(MIX, gated=0)), ("down_1", dict(NORM, mm=0, gated=0, z=KC))],
            "branch": [(f"branch_{l}", dict(mm=48, gates=24, merged=24)) for l in range(DEPTH)],
            "ffn": [(f"ffn_{l}", dict(mm=2 * FC, silu=FC, hid=FC)) for l in range(DEPTH)],
        }
        family = {tag: f for f, L in FAMILIES.items() for tag, _ in L}

        def sig(tag, what):
            return sem(f"{family[tag]}_{what}")

        def at(tag, what, v):
            base = 0
            for t, totals in FAMILIES[family[tag]]:
                if t == tag:
                    return sig(tag, what), base + v
                base += totals[what]

        @block.tensor
        def _(pe):
            taken = [0]

            def take(name):
                seq = taken[0]
                assert tiles[seq][0] == name, (tiles[seq][0], name)
                assert len(used) == seq
                g, slot, n, _ = slot_of(seq)
                pe.wait_ge(loaded(g, slot), 16 * n)
                taken[0] += 1
                return tiles[seq][1](ring[:, slot, :])

            def release(s, v):
                used.append((s, v))

            pe.wait_ge(sem("silu_c"), 1)
            def modulation_tile(l, j):
                w = take(f"mod{l}")
                for m in range(4):
                    for c in range(KC):
                        mm = pe.matmul(MODS_PS[l][:, (4 * j + m) * 2:(4 * j + m) * 2 + 2], w[:, c, m * P:m * P + P],
                                       cc[:, c, :], start=(c == 0), stop=(c == KC - 1))
                mm.then_inc(sem("mods_mm"), 1)
                release(sem("mods_mm"), 12 * l + j + 1)

            for j in range(12):
                modulation_tile(0, j)
            end_stage(pe, "pe")

            def project(tag, L, tile_name, x, wide):
                n_rms = n_rope = 0
                w, cur = None, -1

                def stats(g):
                    nonlocal n_rms
                    if g >= 0 and L[g]["rms"] is not None:
                        pe.wait_ge(*at(tag, "squared", n_rms + 1))
                        if n_rms >= 2:
                            pe.wait_ge(*at(tag, "root", n_rms - 1))
                        pe.matmul(PS[:, 4 + n_rms % 2, 0:512], C("mean_h"), sq_b[:, n_rms % 2, :],
                                  start=True, stop=True).then_inc(sig(tag, "stat"), 1)
                        n_rms += 1

                def rotate(g):
                    nonlocal n_rope
                    if g >= 0 and L[g]["rope"]:
                        pe.wait_ge(*at(tag, "evacuated", g + 1))
                        if L[g]["rms"] is not None:
                            pe.wait_ge(*at(tag, "normed", sum(x["rms"] is not None for x in L[:g + 1])))
                        if n_rope >= 2:
                            pe.wait_ge(*at(tag, "roped", n_rope - 1))
                        pe.matmul(PS[:, 6 + n_rope % 2, 0:TS], C("swap"), L[g]["dst"][:, 0:TS],
                                  start=True, stop=True).then_inc(sig(tag, "rotated"), 1)
                        n_rope += 1

                for g, e in enumerate(L):
                    if e["tile"] != cur:
                        w, cur = take(tile_name), e["tile"]
                    if g >= 4:
                        pe.wait_ge(*at(tag, "evacuated", g - 3))
                    for c in range(KC):
                        if e["kind"] == "f":
                            T = e["n"]
                            o = PS[:, g % 4, 0:T]
                            rhs = x[:, :, c, :] if T == 512 else x[:, 0, c, :]
                            if T == 512:
                                o = o.rearrange("p (s t) -> p s t", s=2)
                            mm = pe.matmul(o, w[:, c, e["m"] * P:e["m"] * P + P], rhs,
                                           start=(c == 0), stop=(c == KC - 1))
                        else:
                            tt = e["tt"]
                            mm = pe.matmul(PS[:, g % 4, 0:e["n"]], x[:, tt // 2, c, (tt % 2) * P:(tt % 2) * P + P],
                                           w[:, c, e["c0"]:e["c0"] + e["n"]], start=(c == 0), stop=(c == KC - 1))
                    mm.then_inc(sig(tag, "mm"), 1)
                    if g + 1 == len(L) or L[g + 1]["tile"] != cur:
                        release(*at(tag, "mm", g + 1))
                    stats(g - 1)
                    rotate(g - 2)
                stats(len(L) - 1)
                rotate(len(L) - 2)
                rotate(len(L) - 1)
                end_stage(pe, "pe")

            def attention(stage):
                U, cu = UNITS[stage], comp_unit[stage]
                for i in range(len(U) + 3):
                    if i < len(U):
                        u = U[i]
                        for k, (q, kk) in enumerate(u["comps"]):
                            j = u["j0"] + k
                            if j >= 4:
                                pe.wait_ge(*at(stage, "exp", j - 3))
                            pe.matmul(PS[:, j % 4, 0:u["n"]], q, kk, start=True, stop=True)\
                              .then_inc(sig(stage, "scores"), 1)
                    if 0 <= i - 2 < len(U):
                        v = i - 2
                        u = U[v]
                        pe.wait_ge(*at(stage, "probs", v + 1))
                        if v >= 2:
                            pe.wait_ge(*at(stage, "turned", v - 1))
                        for kc in range(u["n"] // P):
                            mm = pe.transpose(PS[:, 4 + v % 2, kc * P:kc * P + P],
                                              UB["Pm"][:, u["j0"] % 4, kc * P:kc * P + P], ident)
                        mm.then_inc(sig(stage, "transposed"), 1)
                    if 0 <= i - 3 < len(U):
                        v = i - 3
                        u = U[v]
                        pe.wait_ge(*at(stage, "turned", v + 1))
                        if v >= NO[stage]:
                            pe.wait_ge(*at(stage, "out", v - NO[stage] + 1))
                        nk = u["n"] // P
                        for kc in range(nk):
                            mm = pe.matmul(PS[u["pb"]:u["pb"] + u["dv"], 6 + v % NO[stage], 0:P], u["v"][kc],
                                           UB["PT"][:, v % 2, kc * P:kc * P + P], start=(kc == 0), stop=(kc == nk - 1))
                        mm.then_inc(sig(stage, "pv"), 1)
                    if stage == "att0" and i % 4 == 3 and i // 4 < 12:
                        modulation_tile(1, i // 4)
                end_stage(pe, "pe")

            UB = att_bufs(ATT)

            def subln():
                for m in range(4):
                    pe.wait_ge(sem("subln_squared"), m + 1)
                    pe.matmul(PS[:, m, :], C("mean_p"), carve(m * 512, 512), start=True, stop=True)\
                      .then_inc(sem("subln_stat"), 1)
                end_stage(pe, "pe")

            def out_proj(tag, tile_name, T, x):
                for g in range(KC):
                    if g % 4 == 0:
                        w = take(tile_name)
                    for c in range(KC):
                        mm = pe.matmul(PS[:, g, 0:T], w[:, c, (g % 4) * P:(g % 4) * P + P], x[:, c, 0:T],
                                       start=(c == 0), stop=(c == KC - 1))
                    mm.then_inc(sig(tag, "mm"), 1)
                    if g % 4 == 3:
                        release(*at(tag, "mm", g + 1))

            def norm(tag, T, per_chunk):
                for c in range(KC):
                    pe.wait_ge(*at(tag, "z", per_chunk(c)))
                    if c == 0:
                        pe.wait_ge(*at(tag, "z", per_chunk(c + 7)))
                    o = PS[:, 0, 0:T].rearrange("p (s t) -> p s t", s=2) if T == 512 else PS[:, 0, 0:T]
                    mm = pe.matmul(o, C("mean_d"), hv(T, c), start=(c == 0), stop=(c == KC - 1))
                mm.then_inc(sig(tag, "mean"), 1)
                for c in range(KC):
                    pe.wait_ge(*at(tag, "squared", c + 1))
                    mm = pe.matmul(PS[:, 1, 0:T], C("mean_d"), carve(14848 + (c % 2) * 512, T),
                                   start=(c == 0), stop=(c == KC - 1))
                    mm.then_inc(sig(tag, "var"), 1)
                end_stage(pe, "pe")

            def moe(l):
                T = 512 if l == 0 else TS
                nt = T // P
                pe.wait_ge(sem("router_weights"), 48 * (l + 1))
                for tt in range(nt):
                    for c in range(KC):
                        mm = pe.matmul(PS[:, 0, tt * 36:tt * 36 + 36], a[:, tt // 2, c, (tt % 2) * P:(tt % 2) * P + P],
                                       wgr[:, c, :], start=(c == 0), stop=(c == KC - 1))
                mm.then_inc(sem("logits"), 1)
                for tt in range(nt):
                    for hf in range(2):
                        k = 2 * tt + hf
                        if k >= 4:
                            pe.wait_ge(sem("rows_copied"), k - 3)
                        for c in range(4):
                            mm = pe.transpose(PS[:, 4 + k % 4, c * P:c * P + P],
                                              a[:, tt // 2, 4 * hf + c, (tt % 2) * P:(tt % 2) * P + P], ident)
                        mm.then_inc(sem("rows_turned"), 1)
                pe.wait_ge(sem("chosen"), l + 1)
                both = R["A"][2]
                for tt in range(nt):
                    for t2 in range(tt + 1):
                        pe.matmul(PS[:, 1, tt * NE:tt * NE + NE], C("before") if t2 == tt else C("ones"), both[:, t2, :],
                                  start=(t2 == 0), stop=(t2 == tt))
                for t2 in range(nt):
                    mm = pe.matmul(PS[:, 2, 0:NE], C("ones"), both[:, t2, :], start=(t2 == 0), stop=(t2 == nt - 1))
                mm.then_inc(sem("ranks"), 1)
                pe.wait_ge(sem("routed"), l + 1)
                r0 = SEG[l + 1] % RING

                def take_tokens():
                    for c in range(KC):
                        for tt in range(nt):
                            mm = pe.matmul(PS[:, 0, c * CAP:c * CAP + CAP], X["xrow"][:, tt, c * P:c * P + P],
                                           X["sel"][:, tt, :], start=(tt == 0), stop=(tt == nt - 1))
                    mm.then_inc(sem(f"x_taken{l}"), 1)

                pe.wait_ge(sem("rows_copied"), 8 if l == 0 else 12)
                pe.wait_ge(sem(f"selected{l}"), 1)
                take_tokens()
                pairs = pe.value_load(np_i[0:1, 0:1], min_val=1, max_val=NE // 2)
                with engine_loop(pe, 0, pairs) as i:
                    for s in range(2):
                        w1 = ring[:, (r0 + 3 * s) % RING, :].rearrange("p (c n) -> p c n", c=KC)
                        w3 = ring[:, (r0 + 3 * s + 1) % RING, :].rearrange("p (c n) -> p c n", c=KC)
                        w2 = ring[:, (r0 + 3 * s + 2) % RING, :].rearrange("p (c n) -> p c n", c=4)
                        n = pe.value_load(sub_i[0:1, 0, bass.ds(i * 2 + s, 1)], min_val=1, max_val=8)
                        b0 = pe.value_load(sub_i[0:1, 1, bass.ds(i * 2 + s, 1)], min_val=0, max_val=NBLK - 1)
                        loads = pe.snap(i * 16 + 16)
                        for q in (0, 1):
                            pe.wait_ge(moe_loaded(l, (r0 + 3 * s + q) % RING), loads)
                            pe.sem_inc(sem("pe_step"), 1)
                        with engine_loop(pe, 0, n) as k:
                            j1 = pe.snap(b0 + k + 1)
                            j2 = pe.snap(b0 + k + 2)
                            pe.wait_ge(sem(f"x_ready{l}"), j1)
                            pe.sem_inc(sem("pe_step"), 1)
                            for c in range(KC):
                                pe.matmul(PS[0:CAP, 2, :], X["xe"][:, c, :], w1[:, c, :], start=(c == 0), stop=(c == KC - 1))
                                mm = pe.matmul(PS[CAP:P, 3, :], X["xe"][:, c, :], w3[:, c, :],
                                               start=(c == 0), stop=(c == KC - 1))
                            mm.then_inc(sem(f"w13_done{l}"), 1)
                            pe.wait_ge(sem(f"selected{l}"), j2)
                            pe.sem_inc(sem("pe_step"), 1)
                            take_tokens()
                            pe.wait_ge(sem(f"hidden{l}"), j1)
                            pe.sem_inc(sem("pe_step"), 1)
                            for c in range(4):
                                mm = pe.transpose(PS[:, 4, c * CAP:c * CAP + CAP], X["hid"][0:CAP, c * P:c * P + P],
                                                  ident[0:CAP, 0:CAP])
                            mm.then_inc(sem(f"hidden_turned{l}"), 1)
                            pe.wait_ge(sem(f"hidden_ready{l}"), j1)
                            pe.sem_inc(sem("pe_step"), 1)
                            pe.wait_ge(moe_loaded(l, (r0 + 3 * s + 2) % RING), loads)
                            pe.sem_inc(sem("pe_step"), 1)
                            for c in range(4):
                                for h2 in range(2):
                                    mm = pe.matmul(PS[h2 * CAP:h2 * CAP + CAP, 6 + s, :], X["hidT"][:, c, :],
                                                   w2[:, c, h2 * 512:h2 * 512 + 512], start=(c == 0), stop=(c == 3))
                            mm.then_inc(sem(f"w2_done{l}"), 1)
                end_stage(pe, "pe")
                for tt in range(nt):
                    pe.wait_ge(sem(f"mixed{l}"), tt + 1)
                    for hf in range(2):
                        k = 2 * tt + hf
                        if k >= 4:
                            pe.wait_ge(*at(f"moe{l}", "z", k - 3))
                        for c in range(4):
                            mm = pe.transpose(PS[:, 2 + k % 4, c * P:c * P + P],
                                              X["y1"][:, tt % 2, (4 * hf + c) * P:(4 * hf + c) * P + P], ident)
                        mm.then_inc(sem(f"moe{l}_back"), 1)
                norm(f"moe{l}", T, lambda c: 2 * nt)

            project("proj0", PROJ[0], "in0", a, True)
            attention("att0")
            subln()
            out_proj("mix0", "out0", 512, oT)
            norm("mix0", 512, lambda c: KC)
            moe(0)
            project("proj1", PROJ[1], "in1", a, True)
            attention("att1")
            out_proj("mix1", "out1", TS, o1T)
            norm("mix1", TS, lambda c: KC)
            moe(1)
            for l in range(DEPTH):
                project(f"proj2_{l}", PROJ2, f"in2_{l}", h, False)
                attention(f"att2_{l}")
                tag = f"branch_{l}"
                for b, y in enumerate((ya2, cv2, yc2)):
                    for part in range(2):
                        for m in range(KC):
                            if part == 0 and m % 4 == 0:
                                w = take(f"gate2_{l}")
                            if part == 1 and m == 0:
                                w = take(f"branch2_{l}")
                            g = (2 * b + part) * KC + m
                            if part == 0 and b:
                                pe.wait_ge(*at(tag, "merged", (b - 1) * KC + m + 1))
                            if part == 1:
                                pe.wait_ge(*at(tag, "gates", b * KC + m + 1))
                            n = KC if part == 0 else 4
                            for c in range(n):
                                lhs = w[:, c, (m % 4) * P:(m % 4) * P + P] if part == 0 else w[:, c, m * P:m * P + P]
                                rhs = h[:, 0, c, :] if part == 0 else y[:, c, :]
                                mm = pe.matmul(PS[:, m, 0:TS], lhs, rhs, start=(c == 0), stop=(c == n - 1))
                            mm.then_inc(sig(tag, "mm"), 1)
                            if (part == 0 and m % 4 == 3) or (part == 1 and m == 7):
                                release(*at(tag, "mm", g + 1))
                end_stage(pe, "pe")
                out_proj(f"mix2_{l}", f"out2_{l}", TS, M2)
                norm(f"mix2_{l}", TS, lambda c: KC)
                tag = f"ffn_{l}"
                g = 0
                for j in range(6):
                    nm = min(4, FC - 4 * j)
                    for part, nm_ in ((0, f"ffn_gate_{l}"), (1, f"ffn_up_{l}")):
                        w = take(nm_)
                        for m in range(nm):
                            k = 4 * j + m
                            if j and part == 0:
                                pe.wait_ge(*at(tag, "silu", k - 3))
                            if j and part == 1:
                                pe.wait_ge(*at(tag, "hid", k - 3))
                            for c in range(KC):
                                mm = pe.matmul(PS[:, 4 * part + m, 0:TS], w[:, c, m * P:m * P + P], h[:, 0, c, :],
                                               start=(c == 0), stop=(c == KC - 1))
                            mm.then_inc(sig(tag, "mm"), 1)
                            g += 1
                        release(*at(tag, "mm", g))
                end_stage(pe, "pe")
                for j in range(6):
                    nk = min(4, FC - 4 * j)
                    w = take(f"ffn_down_{l}")
                    for c in range(nk):
                        for m in range(KC):
                            mm = pe.matmul(PS[:, m, 0:TS], w[:, c, m * P:m * P + P], hid2[:, 4 * j + c, :],
                                           start=(j == 0 and c == 0), stop=(4 * j + c == FC - 1))
                    mm.then_inc(sem(f"down_{l}"), 1)
                    release(sem(f"down_{l}"), j + 1)
                norm(f"down_{l}", TS, lambda c: KC)
            assert taken[0] == len(tiles)

        @block.scalar
        def _(act):
            link = Chain(act, "act_link")
            loads = [(cst[:, :], A["consts"]), (h[:, 0], A["xT"]), (h[:, 1], A["ctxT"]),
                     (modb[:, :, :], A["mod_bT"]), (lng[:, :, :], A["ln_gT"]), (lnb[:, :, :], A["ln_bT"]),
                     (lng2[:, :, :], A["ln_g2T"]), (lnb2[:, :, :], A["ln_b2T"]), (subg[:, :], A["sublnT"]),
                     (qkg[0:HD, :], A["qkgT"]), (qkg[HD:P, :], A["qkgT"]),
                     (sinks[:, 0:8], A["win_sink"].to_broadcast([P, 8])),
                     (sinks[:, 8:24], A["attn_sinks"].to_broadcast([P, 16])),
                     (convw[:, :, :, :], A["convT"]), (carve(0, 256), A["diff_lambda"].to_broadcast([P, 256]))]
            act.dma_start(small[:, 0:16], A["cT"]).then_inc(sem("c_loaded"), 16)
            for o, i in loads:
                act.dma_start(o, i).then_inc(sem("params"), 16)
            for dr in range(7):
                act.dma_start(Bd[dr], bass.AP(A["na_rpb"].tensor, (dr + 4) * 31 + 15, [[465, 8], [-1, 64], [1, 64]]))\
                   .then_inc(sem("rpb_spread"), 16)
            act.wait_ge(sem("c_loaded"), 16)
            act.activation(cc[:, :, :], small[:, 0:16].rearrange("p (c s) -> p c s", s=2), ACT.Silu)\
               .then_inc(sem("silu_c"), 1)
            act.wait_ge(sem("params"), 16 * len(loads))
            act.wait_ge(sem("lam_dot"), 1)
            act.activation(neglam[:, 1:3], neglam[:, 1:3], ACT.Exp).then_inc(sem("lam_exp"), 1)
            end_stage(act, "act")

            def project(tag, L, dup, rpb=False):
                if rpb:
                    act.wait_ge(sem("rpb_spread"), 16 * 7)
                    for t in range(2):
                        for r in range(2):
                            for kr in range(4):
                                act.dma_start(rpbT[64 * r:64 * r + 64, t, :, 64 * kr:64 * kr + 64],
                                              Bd[kr - (2 * t + r) + 3].rearrange("h q k -> q h k"))\
                                   .then_inc(sem("rpb_loaded"), 16)
                n_rms = 0

                def root(g):
                    nonlocal n_rms
                    if g >= 0 and L[g]["rms"] is not None:
                        act.wait_ge(*at(tag, "stat", n_rms + 1))
                        if n_rms >= 2:
                            act.wait_ge(*at(tag, "normed", n_rms - 1))
                        act.activation(rs_b[:, n_rms % 2, :], PS[:, 4 + n_rms % 2, :], ACT.Sqrt, bias=C("eps_rms"))\
                           .then_inc(sig(tag, "root"), 1)
                        n_rms += 1

                n_sq = 0
                for g, e in enumerate(L):
                    act.wait_ge(*at(tag, "mm", g + 1))
                    act.activation(e["dst"], PS[:, g % 4, 0:e["n"]], ACT.Copy).then_inc(sig(tag, "evacuated"), 1)
                    if e["rms"] is not None:
                        if n_sq >= 2:
                            act.wait_ge(*at(tag, "stat", n_sq - 1))
                        act.wait_ge(*at(tag, "evacuated", g + 1))
                        act.activation(sq_b[:, n_sq % 2, :], e["dst"], ACT.Square).then_inc(sig(tag, "squared"), 1)
                        n_sq += 1
                    root(g - 1)
                root(len(L) - 1)
                kr, kd, n = dup
                nr = sum(e["rope"] for e in L)
                if nr:
                    act.wait_ge(*at(tag, "roped", nr))
                else:
                    act.wait_ge(*at(tag, "evacuated", len(L)))
                for kv in range(2):
                    for i in range(2):
                        act.activation(kd[halves(i), kv, 0:n], kr[halves(kv), 0:n], ACT.Copy)
                end_stage(act, "act")

            def attention(stage):
                U, cu = UNITS[stage], comp_unit[stage]
                B = att_bufs(ATT)
                for i in range(len(U) + 3):
                    if i < len(U):
                        u = U[i]
                        for j in range(u["j0"], u["j1"]):
                            act.wait_ge(*at(stage, "max", j + 1))
                            if j >= 4:
                                act.wait_ge(*at(stage, "transposed", cu[j - 4] + 1))
                            src = B["Sm"][:, j % 2, 0:u["n"]] if u["mask"] else PS[:, j % 4, 0:u["n"]]
                            if u["sink"] is not None:
                                act.activation(small[:, 24 + j % 8:25 + j % 8], u["sink"], ACT.Exp,
                                               bias=small[:, 8 + j % 8:9 + j % 8])
                            act.activation(B["Pm"][:, j % 4, 0:u["n"]], src, ACT.Exp, bias=small[:, 8 + j % 8:9 + j % 8],
                                           scale=SCALE, accum_out=small[:, 16 + j % 8:17 + j % 8])\
                               .then_inc(sig(stage, "exp"), 1)
                    if 0 <= i - 2 < len(U):
                        v = i - 2
                        act.wait_ge(*at(stage, "transposed", v + 1))
                        if v >= 2:
                            act.wait_ge(*at(stage, "pv", v - 1))
                        act.activation(B["PT"][:, v % 2, 0:U[v]["n"]], PS[:, 4 + v % 2, 0:U[v]["n"]], ACT.Copy)\
                           .then_inc(sig(stage, "turned"), 1)
                    if 0 <= i - 3 < len(U):
                        v = i - 3
                        u = U[v]
                        act.wait_ge(*at(stage, "pv", v + 1))
                        act.activation(u["out"], PS[u["pb"]:u["pb"] + u["dv"], 6 + v % NO[stage], 0:P], ACT.Copy)\
                           .then_inc(sig(stage, "out"), 1)
                end_stage(act, "act")

            def subln():
                for m in range(4):
                    act.activation(carve(m * 512, 512), oT[:, m, :], ACT.Square).then_inc(sem("subln_squared"), 1)
                for m in range(4):
                    act.wait_ge(sem("subln_stat"), m + 1)
                    act.activation(carve(2048 + m * 512, 512), PS[:, m, :], ACT.Sqrt, bias=C("eps_rms"))\
                       .then_inc(sem("subln_root"), 1)
                end_stage(act, "act")

            def gated(tag, l, T):
                for g in range(KC):
                    act.wait_ge(*at(tag, "mm", g + 1))
                    if g >= 2:
                        act.wait_ge(*at(tag, "z", g - 1))
                    for s in range(T // TS):
                        ins = act.activation(carve(13824 + (g % 2) * 512 + s * TS, TS), PS[:, g, s * TS:s * TS + TS],
                                             ACT.Copy, scale=mods[:, l, 2 * KC + g, s:s + 1])
                    ins.then_inc(sig(tag, "gated"), 1)

            def norm(tag, T, gain, bias, extra=None):
                for c in range(KC):
                    act.wait_ge(*at(tag, "centred", c + 1))
                    if c >= 2:
                        act.wait_ge(*at(tag, "var", c - 1))
                    o = carve(14848 + (c % 2) * 512, T)
                    if T == 512:
                        o = o.rearrange("p (s t) -> p s t", s=2)
                    act.activation(o, hv(T, c), ACT.Square).then_inc(sig(tag, "squared"), 1)
                act.wait_ge(*at(tag, "var", KC))
                act.wait_ge(*at(tag, "squared", KC))
                act.activation(carve(14848, T), PS[:, 1, 0:T], ACT.Sqrt, bias=C("eps_ln")).then_inc(sig(tag, "std"), 1)
                for c in range(KC):
                    act.wait_ge(*at(tag, "scaled", c + 1))
                    act.activation(hv(T, c), hv(T, c), ACT.Identity, scale=gain[:, c:c + 1], bias=bias[:, c:c + 1])\
                       .then_inc(sig(tag, "normed"), 1)
                end_stage(act, "act")

            def moe(l):
                T = 512 if l == 0 else TS
                nt = T // P
                act.dma_start(wgr[:, :, 0:4], A["wgT"][:, l]).then_inc(sem("router_weights"), 16)
                act.dma_start(wgr[:, :, 4:36], A["wrT"][:, l]).then_inc(sem("router_weights"), 16)
                act.dma_start(bgr[:, :], A["bgr"][l:l + 1, :].to_broadcast([P, 36])).then_inc(sem("router_weights"), 16)
                for tt in range(nt):
                    for hf in range(2):
                        k = 2 * tt + hf
                        act.wait_ge(sem("rows_turned"), 8 * l + k + 1)
                        act.activation(X["xrow"][:, tt, hf * 512:hf * 512 + 512], PS[:, 4 + k % 4, :], ACT.Copy)\
                           .then_inc(sem("rows_copied"), 1)
                act.wait_ge(sem("group_max"), l + 1)
                act.activation(R["ge"][:, 0:nt, :], R["ge"][:, 0:nt, :], ACT.Exp).then_inc(sem("group_exp"), 1)
                act.wait_ge(sem("pair_diff"), l + 1)
                act.activation(R["f"][:, 2, 0:nt], R["f"][:, 2, 0:nt], ACT.Exp).then_inc(sem("pair_exp"), 1)

                act.wait_ge(sem("routed"), l + 1)

                def tokens_in():
                    act.activation(X["xe"], PS[:, 0, :].rearrange("p (c t) -> p c t", c=KC), ACT.Copy)\
                       .then_inc(sem(f"x_ready{l}"), 1)

                act.wait_ge(sem(f"x_taken{l}"), 1)
                tokens_in()
                pairs = act.value_load(np_i[0:1, 0:1], min_val=1, max_val=NE // 2)
                with engine_loop(act, 0, pairs) as i:
                    for s in range(2):
                        n = act.value_load(sub_i[0:1, 0, bass.ds(i * 2 + s, 1)], min_val=1, max_val=8)
                        b0 = act.value_load(sub_i[0:1, 1, bass.ds(i * 2 + s, 1)], min_val=0, max_val=NBLK - 1)
                        same = act.value_load(sub_i[0:1, 5, bass.ds(i * 2 + s, 1)], min_val=0, max_val=NBLK - 1)
                        with engine_loop(act, 0, n) as k:
                            j1 = act.snap(b0 + k + 1)
                            j2 = act.snap(b0 + k + 2)
                            act.wait_ge(sem(f"w13_done{l}"), j2)
                            act.sem_inc(sem("act_step"), 1)
                            act.activation(X["sil"][CAP:P, :], PS[0:CAP, 2, :], ACT.Silu).then_inc(sem(f"silu{l}"), 1)
                            act.wait_ge(sem(f"x_taken{l}"), j2)
                            act.sem_inc(sem("act_step"), 1)
                            tokens_in()
                            act.wait_ge(sem(f"w2_done{l}"), j2)
                            act.sem_inc(sem("act_step"), 1)
                            act.wait_ge(sem(f"y_stored{l}_{s}"), same * 32 + k * 32 + 32)
                            act.sem_inc(sem("act_step"), 1)
                            act.activation(X["ysb"][:, s, :], PS[:, 6 + s, :], ACT.Copy).then_inc(sem(f"y_copied{l}"), 1)
                            act.wait_ge(sem(f"y_copied{l}"), j2)
                            act.sem_inc(sem("act_step"), 1)
                            for h2 in range(2):
                                act.dma_start(Yd[bass.ds(b0 * CAP + k * CAP, CAP), h2 * 512:h2 * 512 + 512],
                                              X["ysb"][h2 * CAP:h2 * CAP + CAP, s, :]).then_inc(sem(f"y_stored{l}_{s}"), 16)
                for s in range(2):
                    total = act.value_load(sub_i[0:1, 4, 2 + s:3 + s], min_val=2, max_val=NBLK + 1)
                    act.wait_ge(sem(f"y_stored{l}_{s}"), total * 32)
                    act.sem_inc(sem("act_step"), 1)
                act.sem_inc(sem("y_all"), 1)
                end_stage(act, "act")
                norm(f"moe{l}", T, lng[:, 2 * l + 1, :], lnb[:, 2 * l + 1, :])

            project("proj0", PROJ[0], (kraw, kT[:, 4:6, :], 512))
            attention("att0")
            subln()
            gated("mix0", 0, 512)
            norm("mix0", 512, lng[:, 0, :], lnb[:, 0, :])
            moe(0)
            project("proj1", PROJ[1], (kraw, kT[:, 4:6, :], 512), rpb=True)
            attention("att1")
            gated("mix1", 1, TS)
            norm("mix1", TS, lng[:, 2, :], lnb[:, 2, :])
            moe(1)
            for l in range(DEPTH):
                project(f"proj2_{l}", PROJ2, (kraw2, kd2, TS))
                attention(f"att2_{l}")
                tag = f"branch_{l}"
                for b in range(3):
                    for m in range(KC):
                        act.wait_ge(*at(tag, "mm", 2 * b * KC + m + 1))
                        if b:
                            act.wait_ge(*at(tag, "merged", (b - 1) * KC + m + 1))
                        act.activation(G2[:, m, :], PS[:, m, 0:TS], ACT.Sigmoid).then_inc(sig(tag, "gates"), 1)
                end_stage(act, "act")
                norm(f"mix2_{l}", TS, lng2[:, 2 * l, :], lnb2[:, 2 * l, :])
                tag = f"ffn_{l}"
                for k in range(FC):
                    j, m = divmod(k, 4)
                    act.wait_ge(*at(tag, "mm", 8 * j + m + 1))
                    if k >= 4:
                        act.wait_ge(*at(tag, "hid", k - 3))
                    act.activation(sg2[:, m, :], PS[:, m, 0:TS], ACT.Silu).then_inc(sig(tag, "silu"), 1)
                end_stage(act, "act")
                norm(f"down_{l}", TS, lng2[:, 2 * l + 1, :], lnb2[:, 2 * l + 1, :])
            act.dma_start(out, h[:, 0]).then_inc(sem("out_stored"), 16)
            act.wait_ge(sem("out_stored"), 16)

        @block.vector
        def _(dve):
            link = Chain(dve, "dve_link")
            dve.wait_ge(sem("params"), 16 * 15)
            lv = carve(0, 4, HD)
            link(dve.tensor_tensor(carve(256, 2, HD), lv[:, 0:4:2, :], lv[:, 1:4:2, :], ALU.mult))
            dve.tensor_reduce(neglam[:, 1:3], carve(256, 2, HD), AX.X, ALU.add).then_inc(sem("lam_dot"), 1)
            dve.wait_ge(sem("lam_exp"), 1)
            link(dve.tensor_tensor(neglam[:, 3:4], neglam[:, 2:3], neglam[:, 1:2], ALU.subtract))
            link(dve.tensor_scalar(neglam[:, 0:1], neglam[:, 3:4], -LAM_INIT, None, ALU.add))
            def take_mods(l):
                dve.wait_ge(sem("mods_mm"), 12 * (l + 1))
                link(dve.tensor_tensor(mods[:, l, :, :], MODS_PS[l].rearrange("p (j s) -> p j s", s=2),
                                       modb[:, l, :].unsqueeze(2).to_broadcast([P, 48, 2]), ALU.add))
                for k in (1, 4):
                    link(dve.tensor_scalar(mods[:, l, k * KC:k * KC + KC, :], mods[:, l, k * KC:k * KC + KC, :],
                                           1.0, None, ALU.add))

            take_mods(0)

            def modulate(l, shift, T, tag=None):
                for c in range(KC):
                    if tag:
                        dve.wait_ge(*at(tag, "normed", c + 1))
                    for s in range(T // TS):
                        dve.tensor_scalar(a[:, s, c, :], h[:, s, c, :], mods[:, l, (shift + 1) * KC + c, s:s + 1],
                                          mods[:, l, shift * KC + c, s:s + 1], ALU.mult, ALU.add)

            modulate(0, 0, 512)
            end_stage(dve, "dve")

            def project(tag, L):
                n_rms = n_rope = 0
                for g, e in enumerate(L):
                    if e["rms"] is not None:
                        dve.wait_ge(*at(tag, "root", n_rms + 1))
                        link(dve.reciprocal(rs_b[:, n_rms % 2, :], rs_b[:, n_rms % 2, :]))
                        dve.scalar_tensor_tensor(out=e["dst"], in0=e["dst"], scalar=qkg[:, e["rms"]:e["rms"] + 1],
                                                 in1=rs_b[:, n_rms % 2, :], op0=ALU.mult, op1=ALU.mult)\
                           .then_inc(sig(tag, "normed"), 1)
                        n_rms += 1
                    if e["rope"]:
                        d = e["dst"][:, 0:TS]
                        b = rp_b[:, n_rope % 2, :]
                        dve.wait_ge(*at(tag, "rotated", n_rope + 1))
                        dve.tensor_tensor(b, PS[:, 6 + n_rope % 2, 0:TS], C("sin"), ALU.mult)
                        link(dve.tensor_tensor(d, d, C("cos"), ALU.mult))
                        dve.tensor_tensor(d, d, b, ALU.add).then_inc(sig(tag, "roped"), 1)
                        n_rope += 1

            def attention(stage):
                U = UNITS[stage]
                B = att_bufs(ATT)
                S8 = lambda base, j: small[:, base + j % 8:base + j % 8 + 1]
                for i in range(len(U) + 1):
                    if i < len(U):
                        u = U[i]
                        n = u["n"]
                        for j in range(u["j0"], u["j1"]):
                            dve.wait_ge(*at(stage, "scores", j + 1))
                            src = PS[:, j % 4, 0:n]
                            if u["mask"]:
                                if j >= 2:
                                    dve.wait_ge(*at(stage, "exp", j - 1))
                                mk, mn, mul = u["mask"]
                                if mn < n:
                                    dve.tensor_copy(B["Sm"][:, j % 2, mn:n], PS[:, j % 4, mn:n])
                                link(dve.scalar_tensor_tensor(out=B["Sm"][:, j % 2, 0:mn], in0=mk, scalar=mul,
                                                              in1=PS[:, j % 4, 0:mn], op0=ALU.mult, op1=ALU.add))
                                src = B["Sm"][:, j % 2, 0:n]
                            got_max = link.mark(dve.tensor_reduce(S8(0, j), src, AX.X, ALU.max))
                    if i >= 1:
                        pu = U[i - 1]
                        for j in range(pu["j0"], pu["j1"]):
                            dve.wait_ge(*at(stage, "exp", j + 1))
                            if pu["sink"] is not None:
                                link(dve.tensor_tensor(S8(16, j), S8(16, j), S8(24, j), ALU.add))
                            got_sum = link.mark(dve.reciprocal(S8(32, j), S8(16, j)))
                    if i < len(U):
                        link.wait(got_max)
                        for j in range(u["j0"], u["j1"]):
                            if u["sink"] is not None:
                                link(dve.tensor_scalar(S8(0, j), S8(0, j), SCALE, u["sink"], ALU.mult, ALU.max))
                                dve.tensor_scalar(S8(8, j), S8(0, j), -1.0, None, ALU.mult).then_inc(sig(stage, "max"), 1)
                            else:
                                dve.tensor_scalar(S8(8, j), S8(0, j), -SCALE, None, ALU.mult).then_inc(sig(stage, "max"), 1)
                    if i >= 1:
                        link.wait(got_sum)
                        n, j = pu["n"], pu["j0"]
                        p = B["Pm"][:, j % 4, 0:n]
                        if not pu["diff"]:
                            dve.tensor_scalar(p, p, S8(32, j), None, ALU.mult).then_inc(sig(stage, "probs"), 1)
                        else:
                            scaled = link.mark(dve.tensor_scalar(S8(40, j + 1), S8(32, j + 1), neglam[:, 0:1], None, ALU.mult))
                            done = link.mark(dve.tensor_scalar(p, p, S8(32, j), None, ALU.mult))
                            link.wait(done)
                            dve.scalar_tensor_tensor(out=p, in0=B["Pm"][:, (j + 1) % 4, 0:n], scalar=S8(40, j + 1), in1=p,
                                                     op0=ALU.mult, op1=ALU.add).then_inc(sig(stage, "probs"), 1)
                if stage == "att0":
                    take_mods(1)
                end_stage(dve, "dve")

            def subln():
                for m in range(4):
                    dve.wait_ge(sem("subln_root"), m + 1)
                    r = carve(2048 + m * 512, 512)
                    link(dve.reciprocal(r, r))
                    link(dve.scalar_tensor_tensor(out=oT[:, m, :], in0=oT[:, m, :], scalar=subg[:, 0:1], in1=r,
                                                  op0=ALU.mult, op1=ALU.mult))
                    dve.tensor_scalar(oT[:, m, :], oT[:, m, :], 1.0 - LAM_INIT, None, ALU.mult)
                end_stage(dve, "dve")

            def residual(tag, T, gated):
                for g in range(KC):
                    if gated:
                        dve.wait_ge(*at(tag, "gated", g + 1))
                        o = carve(13824 + (g % 2) * 512, T)
                    else:
                        dve.wait_ge(*at(tag, "mm", g + 1))
                        o = PS[:, g, 0:T]
                    if T == 512:
                        o = o.rearrange("p (s t) -> p s t", s=2)
                    dve.scalar_tensor_tensor(out=hv(T, g), in0=hv(T, g), scalar=ALPHA, in1=o, op0=ALU.mult, op1=ALU.add)\
                       .then_inc(sig(tag, "z"), 1)

            def norm(tag, T):
                dve.wait_ge(*at(tag, "mean", 1))
                o = PS[:, 0, 0:T]
                if T == 512:
                    o = o.rearrange("p (s t) -> p s t", s=2)
                for c in range(KC):
                    dve.tensor_tensor(hv(T, c), hv(T, c), o, ALU.subtract).then_inc(sig(tag, "centred"), 1)
                dve.wait_ge(*at(tag, "std", 1))
                link(dve.reciprocal(carve(14848, T), carve(14848, T)))
                r = carve(14848, T)
                if T == 512:
                    r = r.rearrange("p (s t) -> p s t", s=2)
                for c in range(KC):
                    dve.tensor_tensor(hv(T, c), hv(T, c), r, ALU.mult).then_inc(sig(tag, "scaled"), 1)

            def moe(l):
                T = 512 if l == 0 else TS
                nt = T // P
                L, f, A3 = R["L"][:, 0:nt], R["f"], R["A"]
                dve.wait_ge(sem("router_weights"), 48 * (l + 1))
                dve.wait_ge(sem("logits"), l + 1)
                link(dve.tensor_tensor(L, PS[:, 0, 0:36 * nt].rearrange("p (t e) -> p t e", e=36),
                                       bgr[:, :].unsqueeze(1).to_broadcast([P, nt, 36]), ALU.add))
                link(dve.memset(R["g8"][:, 0:nt, :], NEG))
                link(dve.tensor_copy(R["g8"][:, 0:nt, 0:4], L[:, :, 0:4]))
                for t in range(nt):
                    link(dve.max(R["gmx"][:, t, :], R["g8"][:, t, :]))
                    link(dve.max_index(gidx[:, t, :], R["gmx"][:, t, :], R["g8"][:, t, :]))
                dve.tensor_tensor(R["ge"][:, 0:nt, :], L[:, :, 0:4], R["gmx"][:, 0:nt, 0:1].to_broadcast([P, nt, 4]),
                                  ALU.subtract).then_inc(sem("group_max"), 1)
                link(dve.tensor_copy(f[:, 0, 0:nt], gidx[:, 0:nt, 0]))
                link(dve.tensor_tensor(R["ohg"][:, 0:nt, :], C("iota")[:, 0:4].unsqueeze(1).to_broadcast([P, nt, 4]),
                                       f[:, 0, 0:nt].unsqueeze(2).to_broadcast([P, nt, 4]), ALU.is_equal))
                em = R["em"][:, 0:nt, :].rearrange("p t (g e) -> p t g e", g=4)
                for t in range(nt):
                    link(dve.tensor_tensor(em[:, t], L[:, t, 4:36].rearrange("p (g e) -> p g e", g=4),
                                           R["ohg"][:, t, :].unsqueeze(2).to_broadcast([P, 4, 8]), ALU.mult))
                link(dve.tensor_scalar(R["ohg"][:, 0:nt, :], R["ohg"][:, 0:nt, :], -NEG, NEG, ALU.mult, ALU.add))
                for t in range(nt):
                    link(dve.tensor_tensor(em[:, t], em[:, t], R["ohg"][:, t, :].unsqueeze(2).to_broadcast([P, 4, 8]), ALU.add))
                    link(dve.max(R["emx"][:, t, :], R["em"][:, t, :]))
                    link(dve.max_index(eidx[:, t, :], R["emx"][:, t, :], R["em"][:, t, :]))
                dve.tensor_tensor(f[:, 2, 0:nt], R["emx"][:, 0:nt, 1], R["emx"][:, 0:nt, 0], ALU.subtract)\
                   .then_inc(sem("pair_diff"), 1)
                for k in range(2):
                    link(dve.tensor_copy(f[:, 4 + k, 0:nt], eidx[:, 0:nt, k]))
                    link(dve.tensor_tensor(A3[k][:, 0:nt, :], C("iota")[:, 0:NE].unsqueeze(1).to_broadcast([P, nt, NE]),
                                           f[:, 4 + k, 0:nt].unsqueeze(2).to_broadcast([P, nt, NE]), ALU.is_equal))
                dve.tensor_tensor(A3[2][:, 0:nt, :], A3[0][:, 0:nt, :], A3[1][:, 0:nt, :], ALU.add)\
                   .then_inc(sem("chosen"), 1)
                dve.wait_ge(sem("group_exp"), l + 1)
                link(dve.tensor_reduce(f[:, 3, 0:nt], R["ge"][:, 0:nt, :], AX.X, ALU.add))
                link(dve.reciprocal(f[:, 3, 0:nt], f[:, 3, 0:nt]))
                dve.wait_ge(sem("pair_exp"), l + 1)
                link(dve.tensor_scalar(f[:, 6, 0:nt], f[:, 2, 0:nt], 1.0, None, ALU.add))
                link(dve.reciprocal(f[:, 6, 0:nt], f[:, 6, 0:nt]))
                link(dve.tensor_tensor(w12[:, 0, 0:nt], f[:, 6, 0:nt], f[:, 3, 0:nt], ALU.mult))
                link(dve.tensor_tensor(w12[:, 1, 0:nt], f[:, 2, 0:nt], w12[:, 0, 0:nt], ALU.mult))
                dve.wait_ge(sem("ranks"), l + 1)
                cnt = PS[:, 2, 0:NE]
                link(dve.tensor_scalar(R["has"], cnt, 0.0, None, ALU.is_gt))
                link(dve.tensor_copy(R["ovf"], R["has"]))
                for k in range(1, 8):
                    link(dve.tensor_scalar(R["ob"], cnt, float(k * CAP), None, ALU.is_gt))
                    link(dve.tensor_tensor(R["ovf"], R["ovf"], R["ob"], ALU.add))

                def running(src):
                    link(dve.memset(R["cum"][:, 0:16], 0.0))
                    link(dve.memset(R["cum2"][:, 0:16], 0.0))
                    link(dve.tensor_copy(R["cum"][:, 16:48], src))
                    x, y = R["cum"], R["cum2"]
                    for sh in (1, 2, 4, 8, 16):
                        link(dve.tensor_tensor(y[:, 16:48], x[:, 16:48], x[:, 16 - sh:48 - sh], ALU.add))
                        x, y = y, x
                    return x[:, 16:48]

                F2 = R["subf"]
                end = running(R["has"])
                link(dve.tensor_tensor(R["pos"], end, R["has"], ALU.subtract))
                link(dve.tensor_copy(f[:, 12, 0:1], end[:, NE - 1:NE]))
                end = running(R["ovf"])
                link(dve.tensor_tensor(R["ob"], end, R["ovf"], ALU.subtract))
                link(dve.tensor_copy(f[:, 12, 1:2], end[:, NE - 1:NE]))

                def over_places(x):
                    return x.unsqueeze(1).to_broadcast([P, NT, NE])

                place = C("place").unsqueeze(2).to_broadcast([P, NT, NE])
                at_place, t3 = carve(7680, NT, NE), carve(8768, NT, NE)
                link(dve.tensor_tensor(t3, over_places(R["pos"]), place, ALU.is_lt))
                link(dve.tensor_tensor(t3, t3, over_places(R["ovf"]), ALU.mult))
                link(dve.tensor_reduce(F2[:, 1, :], t3, AX.X, ALU.add))
                link(dve.tensor_tensor(at_place[:, 0:NE, 0:16], R["pos"].unsqueeze(2).to_broadcast([P, NE, 16]),
                                       C("place")[:, 1:33:2].unsqueeze(1).to_broadcast([P, NE, 16]), ALU.is_equal))
                link(dve.tensor_reduce(R["par"], at_place[:, 0:NE, 0:16], AX.X, ALU.add))
                link(dve.tensor_tensor(at_place, over_places(R["par"]),
                                       C("odd_place").unsqueeze(2).to_broadcast([P, NT, NE]), ALU.is_equal))
                link(dve.tensor_tensor(t3, t3, at_place, ALU.mult))
                link(dve.tensor_reduce(F2[:, 5, :], t3, AX.X, ALU.add))
                link(dve.tensor_tensor(at_place, over_places(R["pos"]), place, ALU.is_equal))
                link(dve.tensor_tensor(at_place, at_place, over_places(R["has"]), ALU.mult))
                link(dve.tensor_tensor(t3, at_place, over_places(R["ovf"]), ALU.mult))
                link(dve.tensor_reduce(F2[:, 0, :], t3, AX.X, ALU.add))
                link(dve.tensor_scalar(F2[:, 0, :], F2[:, 0, :], 1.0, None, ALU.max))
                link(dve.tensor_tensor(t3, at_place, over_places(C("iota")[:, 0:NE]), ALU.mult))
                link(dve.tensor_reduce(F2[:, 2, :], t3, AX.X, ALU.add))
                link(dve.memset(F2[:, 3, 0:1], 1.0))
                link(dve.tensor_scalar(F2[:, 3, 1:NT], F2[:, 1, 0:NT - 1], 1.0, None, ALU.add))
                link(dve.tensor_scalar(t3[:, 0, 0:16], C("iota")[:, 0:32:2], f[:, 12, 0:1], None, ALU.is_lt))
                link(dve.tensor_reduce(f[:, 13, 0:1], t3[:, 0, 0:16], AX.X, ALU.add))
                link(dve.tensor_scalar(f[:, 13, 1:2], f[:, 13, 0:1], 2.0, -1.0, ALU.mult, ALU.add))
                link(dve.tensor_scalar(t3[:, 0, :], R["pos"], f[:, 13, 1:2], None, ALU.is_lt))
                link(dve.tensor_tensor(t3[:, 0, :], t3[:, 0, :], R["ovf"], ALU.mult))
                link(dve.memset(F2[:, 4, :], 0.0))
                link(dve.tensor_reduce(f[:, 13, 2:3], t3[:, 0, :], AX.X, ALU.add))
                link(dve.tensor_scalar(F2[:, 4, 0:1], f[:, 13, 2:3], 1.0, None, ALU.add))
                link(dve.tensor_tensor(f[:, 13, 3:4], f[:, 13, 1:2], f[:, 12, 0:1], ALU.subtract))
                link(dve.tensor_tensor(f[:, 13, 3:4], f[:, 13, 3:4], f[:, 12, 1:2], ALU.add))
                link(dve.tensor_scalar(F2[:, 4, 1:2], f[:, 13, 3:4], 2.0, None, ALU.add))
                link(dve.tensor_tensor(t3[:, 0, :], R["par"], R["ovf"], ALU.mult))
                link(dve.tensor_reduce(f[:, 14, 0:1], t3[:, 0, :], AX.X, ALU.add))
                link(dve.tensor_tensor(f[:, 14, 1:2], f[:, 12, 1:2], f[:, 14, 0:1], ALU.subtract))
                link(dve.tensor_scalar(F2[:, 4, 2:3], f[:, 14, 1:2], 1.0, None, ALU.add))
                link(dve.tensor_tensor(F2[:, 4, 3:4], F2[:, 4, 1:2], f[:, 14, 1:2], ALU.subtract))
                link(dve.tensor_copy(np_i[0:1, 0:1], f[0:1, 13, 0:1]))
                dve.tensor_copy(sub_i[0:1, :, :], F2[0:1, :, :]).then_inc(sem("routed"), 1)
                for k in range(2):
                    r, o = f[:, 7, 0:nt], f[:, 8, 0:nt]
                    link(dve.tensor_tensor(R["tmp"][:, 0:nt, :], A3[k][:, 0:nt, :],
                                           PS[:, 1, 0:NE * nt].rearrange("p (t e) -> p t e", e=NE), ALU.mult))
                    link(dve.tensor_reduce(r, R["tmp"][:, 0:nt, :], AX.X, ALU.add))
                    link(dve.tensor_tensor(R["tmp"][:, 0:nt, :], A3[k][:, 0:nt, :],
                                           R["ob"].unsqueeze(1).to_broadcast([P, nt, NE]), ALU.mult))
                    link(dve.tensor_reduce(o, R["tmp"][:, 0:nt, :], AX.X, ALU.add))
                    link(dve.scalar_tensor_tensor(out=R["dd"][:, k, 0:nt], in0=o, scalar=float(CAP), in1=r,
                                                  op0=ALU.mult, op1=ALU.add))
                    link(dve.tensor_copy(dest_i[:, k, 0:nt], R["dd"][:, k, 0:nt]))
                dve.wait_ge(sem("routed"), l + 1)

                def place_first(k, tt):
                    return dve.tensor_scalar(X["sel"][:, tt, :], C("iota"), R["dd"][:, 0, tt:tt + 1], None, ALU.is_equal)

                def place_second(tt):
                    return dve.scalar_tensor_tensor(out=X["sel"][:, tt, :], in0=C("iota"), scalar=R["dd"][:, 1, tt:tt + 1],
                                                    in1=X["sel"][:, tt, :], op0=ALU.is_equal, op1=ALU.add)

                for tt in range(nt):
                    link(place_first(0, tt))
                for tt in range(nt):
                    ins = place_second(tt)
                ins.then_inc(sem(f"selected{l}"), 1)
                pairs = dve.value_load(np_i[0:1, 0:1], min_val=1, max_val=NE // 2)
                with engine_loop(dve, 0, pairs) as i:
                    for s in range(2):
                        n = dve.value_load(sub_i[0:1, 0, bass.ds(i * 2 + s, 1)], min_val=1, max_val=8)
                        b0 = dve.value_load(sub_i[0:1, 1, bass.ds(i * 2 + s, 1)], min_val=0, max_val=NBLK - 1)
                        with engine_loop(dve, 0, n) as k:
                            j1 = dve.snap(b0 + k + 1)
                            j2 = dve.snap(b0 + k + 2)
                            dve.wait_ge(sem(f"x_taken{l}"), j1)
                            dve.sem_inc(sem("dve_step"), 1)
                            dve.tensor_scalar(R["dd"], R["dd"], float(CAP), None, ALU.subtract)\
                               .then_inc(sem(f"slots_moved{l}"), 1)
                            dve.wait_ge(sem(f"slots_moved{l}"), j1)
                            dve.sem_inc(sem("dve_step"), 1)
                            for tt in range(nt):
                                ins = place_first(0, tt)
                            ins.then_inc(sem(f"first_placed{l}"), 1)
                            dve.wait_ge(sem(f"first_placed{l}"), j1)
                            dve.sem_inc(sem("dve_step"), 1)
                            for tt in range(nt):
                                ins = place_second(tt)
                            ins.then_inc(sem(f"selected{l}"), 1)
                            dve.wait_ge(sem(f"silu{l}"), j1)
                            dve.sem_inc(sem("dve_step"), 1)
                            dve.tensor_tensor(X["hid"][0:CAP, :], X["sil"][CAP:P, :], PS[CAP:P, 3, :], ALU.mult)\
                               .then_inc(sem(f"hidden{l}"), 1)
                            dve.wait_ge(sem(f"hidden_turned{l}"), j1)
                            dve.sem_inc(sem("dve_step"), 1)
                            dve.tensor_copy(X["hidT"], PS[:, 4, 0:4 * CAP].rearrange("p (c t) -> p c t", c=4))\
                               .then_inc(sem(f"hidden_ready{l}"), 1)
                end_stage(dve, "dve")
                for tt in range(nt):
                    b = tt % 2
                    dve.wait_ge(sem(f"y_gathered{l}_{b}"), 32 * (tt // 2 + 1))
                    link(dve.tensor_scalar(X["y1"][:, b, :], X["y1"][:, b, :], w12[:, 0, tt:tt + 1], None, ALU.mult))
                    dve.scalar_tensor_tensor(out=X["y1"][:, b, :], in0=X["y2"][:, b, :], scalar=w12[:, 1, tt:tt + 1],
                                             in1=X["y1"][:, b, :], op0=ALU.mult, op1=ALU.add).then_inc(sem(f"mixed{l}"), 1)
                    for hf in range(2):
                        k = 2 * tt + hf
                        dve.wait_ge(sem(f"moe{l}_back"), k + 1)
                        ps = PS[:, 2 + k % 4, :].rearrange("p (c t) -> p c t", c=4)
                        tz = X["tz"][:, k % 2, :].rearrange("p (c t) -> p c t", c=4)
                        s = tt // 2
                        hh = h[:, s, 4 * hf:4 * hf + 4, (tt % 2) * P:(tt % 2) * P + P]
                        gate = mods[:, l, 5 * KC + 4 * hf:5 * KC + 4 * hf + 4, s:s + 1]
                        link(dve.tensor_tensor(tz, ps, gate.to_broadcast([P, 4, P]), ALU.mult))
                        dve.scalar_tensor_tensor(out=hh, in0=hh, scalar=ALPHA, in1=tz, op0=ALU.mult, op1=ALU.add)\
                           .then_inc(sig(f"moe{l}", "z"), 1)
                norm(f"moe{l}", T)
                if l == 0:
                    modulate(1, 0, 512, "moe0")
                end_stage(dve, "dve")

            project("proj0", PROJ[0])
            end_stage(dve, "dve")
            attention("att0")
            subln()
            residual("mix0", 512, True)
            norm("mix0", 512)
            modulate(0, 3, 512, "mix0")
            end_stage(dve, "dve")
            moe(0)
            project("proj1", PROJ[1])
            dve.wait_ge(sem("rpb_loaded"), 16 * 16)
            for hn in range(8):
                dve.scalar_tensor_tensor(out=rpbT[:, :, hn, :], in0=rpbT[:, :, hn, :], scalar=1.0 / SCALE,
                                         in1=CR("nbhd", 2), op0=ALU.mult, op1=ALU.add)
            end_stage(dve, "dve")
            attention("att1")
            residual("mix1", TS, True)
            norm("mix1", TS)
            modulate(1, 3, TS, "mix1")
            end_stage(dve, "dve")
            moe(1)
            for l in range(DEPTH):
                dve.wait_ge(*at(f"proj2_{l}", "evacuated", 19))
                link(dve.tensor_tensor(bc2, bc2, bh2, ALU.mult))
                for m in range(4):
                    u, o = bc2[:, m, :], cv2[:, m, :]
                    link(dve.tensor_scalar(o, u, convw[:, l, 2, m:m + 1], None, ALU.mult))
                    link(dve.scalar_tensor_tensor(out=o[:, 1:TS], in0=u[:, 0:TS - 1], scalar=convw[:, l, 1, m:m + 1],
                                                  in1=o[:, 1:TS], op0=ALU.mult, op1=ALU.add))
                    link(dve.scalar_tensor_tensor(out=o[:, 2:TS], in0=u[:, 0:TS - 2], scalar=convw[:, l, 0, m:m + 1],
                                                  in1=o[:, 2:TS], op0=ALU.mult, op1=ALU.add))
                dve.tensor_tensor(cv2, cv2, bb2, ALU.mult)
                end_stage(dve, "dve")
                attention(f"att2_{l}")
                tag = f"branch_{l}"
                for b in range(3):
                    for m in range(KC):
                        dve.wait_ge(*at(tag, "gates", b * KC + m + 1))
                        dve.wait_ge(*at(tag, "mm", (2 * b + 1) * KC + m + 1))
                        if b == 0:
                            dve.tensor_tensor(M2[:, m, :], G2[:, m, :], PS[:, m, 0:TS], ALU.mult)\
                               .then_inc(sig(tag, "merged"), 1)
                        else:
                            link(dve.tensor_tensor(mt2[:, m % 2, :], G2[:, m, :], PS[:, m, 0:TS], ALU.mult))
                            dve.tensor_tensor(M2[:, m, :], M2[:, m, :], mt2[:, m % 2, :], ALU.add)\
                               .then_inc(sig(tag, "merged"), 1)
                end_stage(dve, "dve")
                residual(f"mix2_{l}", TS, False)
                norm(f"mix2_{l}", TS)
                end_stage(dve, "dve")
                tag = f"ffn_{l}"
                for k in range(FC):
                    j, m = divmod(k, 4)
                    nm = min(4, FC - 4 * j)
                    dve.wait_ge(*at(tag, "silu", k + 1))
                    dve.wait_ge(*at(tag, "mm", 8 * j + nm + m + 1))
                    dve.tensor_tensor(hid2[:, k, :], sg2[:, m, :], PS[:, 4 + m, 0:TS], ALU.mult).then_inc(sig(tag, "hid"), 1)
                end_stage(dve, "dve")
                dve.wait_ge(sem(f"down_{l}"), 6)
                for g in range(KC):
                    dve.scalar_tensor_tensor(out=h[:, 0, g, :], in0=h[:, 0, g, :], scalar=ALPHA, in1=PS[:, g, 0:TS],
                                             op0=ALU.mult, op1=ALU.add).then_inc(sig(f"down_{l}", "z"), 1)
                norm(f"down_{l}", TS)
                end_stage(dve, "dve")

        @block.gpsimd
        def _(pool):
            link = Chain(pool, "pool_link")

            def idle(n):
                for _ in range(n):
                    end_stage(pool, "pool")

            def moe(l):
                T = 512 if l == 0 else TS
                nt = T // P
                for s in range(2):
                    pool.sem_inc(sem(f"y_stored{l}_{s}"), 32)
                pool.sem_inc(sem(f"y_copied{l}"), 1)
                pool.sem_inc(sem(f"w13_done{l}"), 1)
                pool.sem_inc(sem(f"w2_done{l}"), 1)
                end_stage(pool, "pool")
                pool.wait_ge(sem("y_all"), l + 1)
                for tt in range(nt):
                    b = tt % 2
                    if tt >= 2:
                        pool.wait_ge(sem(f"moe{l}_back"), 2 * (tt - 1))
                    for k, y in enumerate((X["y1"], X["y2"])):
                        pool.indirect_dma_start(out=y[:, b, :], out_offset=None, in_=Yd[0:NBLK * CAP, :],
                                                in_offset=bass.IndirectOffsetOnAxis(ap=dest_i[:, k, tt:tt + 1], axis=0))\
                            .then_inc(sem(f"y_gathered{l}_{b}"), 16)
                end_stage(pool, "pool")

            idle(4)
            pool.memset(carve(0, 2 * D), 0.0).then_inc(sem("zero_rows"), 1)
            pool.wait_ge(sem("zero_rows"), 1)
            for b in range(NBLK * CAP // 256):
                pool.dma_start(Yd[b * 256:b * 256 + 256, :].rearrange("(p r) n -> p (r n)", p=P), carve(0, 2 * D))\
                    .then_inc(sem("blocks_zeroed"), 16)
            pool.wait_ge(sem("blocks_zeroed"), 16 * (NBLK * CAP // 256))
            idle(1)
            moe(0)
            idle(3)
            moe(1)
            idle(2 * 6)

        @block.sync
        def _(sp):
            def load(seq):
                g, slot, n, k = slot_of(seq)
                name, view, src = tiles[seq]
                sp.dma_start(view(ring[:, slot, :]), src).then_inc(loaded(g, slot), 16)

            def expert(l, s, e, r0):
                for k, w in enumerate(("moe_w1", "moe_w3", "moe_w2")):
                    c = 4 if k == 2 else KC
                    if isinstance(e, int):
                        src = A[w][l, e].rearrange("(c p) n -> p c n", c=c)
                    else:
                        src = A[w][l, bass.ds(e, 1)].rearrange("a (c p) n -> p (a c) n", c=c)
                    yield k, ring[:, (r0 + 3 * s + k) % RING, :].rearrange("p (c n) -> p c n", c=c), src

            sp.wait_ge(sem("c_loaded"), 16)
            for g in range(3):
                for seq in range(SEG[g], SEG[g + 1]):
                    k = seq - SEG[g]
                    if g == 0 and k >= RING:
                        sp.wait_ge(*used[seq - RING])
                    elif g > 0 and k < RING:
                        l = g - 1
                        if k in (0, 3):
                            done = sp.value_load(sub_i[0:1, 4, k // 3:k // 3 + 1], min_val=1, max_val=NBLK + 1)
                        what = "w2_done" if k % 3 == 2 else "w13_done"
                        sp.wait_ge(sem(f"{what}{l}"), done)
                    elif g > 0:
                        sp.wait_ge(*used[seq - RING])
                    load(seq)
                if g < 2:
                    l, r0 = g, SEG[g + 1] % RING
                    for seq in range(SEG[g + 1] - RING, SEG[g + 1]):
                        sp.wait_ge(*used[seq])
                    sp.wait_ge(sem("routed"), l + 1)
                    pairs = sp.value_load(np_i[0:1, 0:1], min_val=1, max_val=NE // 2)
                    with engine_loop(sp, 0, pairs) as i:
                        for s in range(2):
                            e = sp.value_load(sub_i[0:1, 2, bass.ds(i * 2 + s, 1)], min_val=0, max_val=NE - 1)
                            done = sp.value_load(sub_i[0:1, 3, bass.ds(i * 2 + s, 1)], min_val=1, max_val=NBLK)
                            for k, dst, src in expert(l, s, e, r0):
                                what = "w2_done" if k == 2 else "w13_done"
                                sp.wait_ge(sem(f"{what}{l}"), done)
                                sp.dma_start(dst, src).then_inc(moe_loaded(l, (r0 + 3 * s + k) % RING), 16)


def kernel(**inputs):
    import concourse.bacc as _bacc
    from concourse.bass_utils import run_bass_kernel_spmd as _run

    def get(n):
        return np.asarray(inputs[n])

    def chunks(v):
        v = v.reshape(v.shape[:-1] + (-1, P))
        return np.moveaxis(v, -1, 0)

    arrays = {
        "consts": CONST_ARRAY,
        "cT": np.stack([chunks(get("c")[0]), chunks(get("c_ctx"))], -1).reshape(P, 16),
        "xT": np.swapaxes(chunks(get("x")[0]), 1, 2),
        "ctxT": np.swapaxes(chunks(get("ctx")[0]), 1, 2),
        "mod_w": get("mod_w"), "mod_bT": chunks(get("mod_b")),
        "ln_gT": chunks(get("ln_g").reshape(4, D)), "ln_bT": chunks(get("ln_b").reshape(4, D)),
        "ln_g2T": chunks(np.stack([get("ln1_g_2"), get("ln2_g_2")], 1).reshape(4, D)),
        "ln_b2T": chunks(np.stack([get("ln1_b_2"), get("ln2_b_2")], 1).reshape(4, D)),
        "sublnT": get("diff_subln_g").reshape(P, 1), "qkgT": get("gqa_qk_g")[0].T,
        "win_sink": get("win_sink").reshape(1, 8), "attn_sinks": get("attn_sinks_2").reshape(1, 16),
        "convT": chunks(get("conv_w_2")), "diff_lambda": get("diff_lambda").reshape(1, 256),
        "ab_w_in": get("ab_w_in"), "ab_w_out": get("ab_w_out"), "cd_w_in": get("cd_w_in"), "cd_w_out": get("cd_w_out"),
        "na_rpb": get("na_rpb"),
        "wgT": np.transpose(get("moe_w_group").reshape(DEPTH, KC, P, 4), (2, 0, 1, 3)),
        "wrT": np.transpose(get("moe_w_router").reshape(DEPTH, KC, P, NE), (2, 0, 1, 3)),
        "bgr": np.concatenate([get("moe_b_group"), get("moe_b_router")], 1),
        "moe_w1": get("moe_w1"), "moe_w3": get("moe_w3"), "moe_w2": get("moe_w2"),
        "w_in_2": get("w_in_2"), "w_branch_a_2": get("w_branch_a_2"), "w_branch_b_2": get("w_branch_b_2"),
        "w_branch_c_2": get("w_branch_c_2"), "w_out_2": get("w_out_2"), "w_ffn_gate_2": get("w_ffn_gate_2"),
        "w_ffn_up_2": get("w_ffn_up_2"), "w_ffn_down_2": get("w_ffn_down_2"),
    }
    nc = _bacc.Bacc("TRN2", target_bir_lowering=False, num_devices=1)
    maps, aps = {}, {}
    for name, v in arrays.items():
        v = np.ascontiguousarray(v)
        maps[f"in_{name}"] = v
        aps[name] = nc.dram_tensor(f"in_{name}", v.shape, mybir.dt.from_np(v.dtype), kind="ExternalInput").ap()
    out = nc.dram_tensor("out_dram", (P, KC, TS), F32, kind="ExternalOutput").ap()
    program(nc, aps, out)
    r = _run(nc, [maps], core_ids=[0])
    return np.ascontiguousarray(np.transpose(r.results[0]["out_dram"], (2, 1, 0)).reshape(1, TS, D))
```
